# Optimizing a Trainium2 kernel written in Bass

```python
import jax, jax.numpy as jnp
from jax import lax
import numpy as np

D_MODEL = 2048
BATCH = 1
SEQ = 512
DEPTH = 1

CHUNK = 64
N_MEM = 256
EPS = 1e-6
MAX_OFFSET = 4096
HG_HEADS = 8
HG_DK = 128
HG_DV = 128
HG_KW = HG_HEADS * HG_DK
HG_VW = HG_HEADS * HG_DV
SW_HEADS = 16
SW_KV_HEADS = 4
SW_HD = 64
SW_QW = SW_HEADS * SW_HD
SW_KVW = SW_KV_HEADS * SW_HD
WINDOW = 128
WINDOW_CHUNKS = WINDOW // CHUNK
ROPE_THETA = 10000.0
X_HEADS = 4
X_HD = 128
X_W = X_HEADS * X_HD
D_FF = (((8 * D_MODEL + 2) // 3 + 255) // 256) * 256
IN_WIDTHS = (HG_KW, HG_KW, HG_VW, HG_VW, SW_QW, SW_KVW, SW_KVW, D_MODEL, D_MODEL)
IN_W = sum(IN_WIDTHS)
IN_OFFSETS = tuple(sum(IN_WIDTHS[:j + 1]) for j in range(len(IN_WIDTHS) - 1))

kernel_name = 'hybrid_hgrn2_swa_sink_memxattn_block'

def rmsnorm(x, g):
    xf = x.astype(jnp.float32)
    var = jnp.mean(xf * xf, axis=-1, keepdims=True)
    return (xf * lax.rsqrt(var + EPS)).astype(x.dtype) * g

def rope(t, pos):
    half = t.shape[-1] // 2
    inv = ROPE_THETA ** (-jnp.arange(half, dtype=jnp.float32) / half)
    ang = pos.astype(jnp.float32)[..., None] * inv
    cos = jnp.cos(ang)[:, :, None, :]
    sin = jnp.sin(ang)[:, :, None, :]
    tf = t.astype(jnp.float32)
    t1, t2 = tf[..., :half], tf[..., half:]
    return jnp.concatenate([t1 * cos - t2 * sin, t2 * cos + t1 * sin], axis=-1).astype(t.dtype)

def hgrn2_mixer(q, f_pre, i, g, lb, norm_g):
    B, T, _ = q.shape
    nC = T // CHUNK
    f32 = jnp.float32
    lbf = lb.astype(f32)
    f = lbf + (1.0 - lbf) * jax.nn.sigmoid(f_pre.astype(f32))
    log_f = jnp.log(f)
    k = 1.0 - f

    def heads(t, hd):
        return t.astype(f32).reshape(B, nC, CHUNK, HG_HEADS, hd).transpose(1, 0, 3, 2, 4)

    qc, kc, vc, lc = heads(q, HG_DK), heads(k, HG_DK), heads(i, HG_DV), heads(log_f, HG_DK)
    causal = jnp.tril(jnp.ones((CHUNK, CHUNK), dtype=bool))[None, None, :, :, None]

    def step(S, inp):
        qq, kk, vv, ll = inp
        b = jnp.cumsum(ll, axis=2)
        b_last = b[:, :, -1:, :]
        o_inter = jnp.einsum('bhtd,bhdv->bhtv', qq * jnp.exp(b), S)
        diff = b[:, :, :, None, :] - b[:, :, None, :, :]
        decay = jnp.exp(jnp.where(causal, diff, -jnp.inf))
        A = jnp.einsum('bhtd,bhsd,bhtsd->bhts', qq, kk, decay)
        o_intra = jnp.einsum('bhts,bhsv->bhtv', A, vv)
        S_new = jnp.exp(b_last[:, :, 0, :])[..., None] * S + jnp.einsum(
            'bhsd,bhsv->bhdv', kk * jnp.exp(b_last - b), vv)
        return S_new, o_inter + o_intra

    S0 = jnp.zeros((B, HG_HEADS, HG_DK, HG_DV), f32)
    _, o = lax.scan(step, S0, (qc, kc, vc, lc))
    o = o.transpose(1, 0, 3, 2, 4).reshape(B, T, HG_HEADS, HG_DV)
    o = o * lax.rsqrt(jnp.mean(o * o, axis=-1, keepdims=True) + EPS)
    o = o * norm_g.astype(f32).reshape(HG_HEADS, HG_DV)
    o = o.reshape(B, T, HG_VW) * jax.nn.silu(g.astype(f32))
    return o.astype(q.dtype)

def swa_mixer(q, k, v, pos, sinks):
    B, T, _ = q.shape
    nC = T // CHUNK
    G = SW_HEADS // SW_KV_HEADS
    q = rope(q.reshape(B, T, SW_HEADS, SW_HD), pos)
    k = rope(k.reshape(B, T, SW_KV_HEADS, SW_HD), pos)
    v = v.reshape(B, T, SW_KV_HEADS, SW_HD)
    qb = q.reshape(B, nC, CHUNK, SW_KV_HEADS, G, SW_HD)

    def band(t):
        tc = t.reshape(B, nC, CHUNK, SW_KV_HEADS, SW_HD)
        prev = [jnp.pad(tc, ((0, 0), (j, 0), (0, 0), (0, 0), (0, 0)))[:, :nC]
                for j in range(WINDOW_CHUNKS - 1, 0, -1)]
        return jnp.concatenate(prev + [tc], axis=2)

    kb, vb = band(k), band(v)
    s = jnp.einsum('bnqhgd,bnkhd->bnhgqk', qb, kb).astype(jnp.float32) * (SW_HD ** -0.5)
    key_chunk = (jnp.arange(nC)[:, None] - (WINDOW_CHUNKS - 1)
                 + jnp.arange(WINDOW_CHUNKS * CHUNK)[None, :] // CHUNK)
    valid = key_chunk >= 0
    s = jnp.where(valid[None, :, None, None, None, :], s, -jnp.inf)
    sink = sinks.astype(jnp.float32).reshape(SW_KV_HEADS, G)[None, None, :, :, None, None]
    sink = jnp.broadcast_to(sink, s.shape[:-1] + (1,))
    p = jax.nn.softmax(jnp.concatenate([s, sink], axis=-1), axis=-1)[..., :-1]
    o = jnp.einsum('bnhgqk,bnkhd->bnqhgd', p.astype(v.dtype), vb)
    return o.reshape(B, T, SW_QW)

def cross_attn(h, mem_n, wq, wk, wv, wo):
    B, T, _ = h.shape
    M = mem_n.shape[1]
    q = (h @ wq).reshape(B, T, X_HEADS, X_HD)
    k = (mem_n @ wk).reshape(B, M, X_HEADS, X_HD)
    v = (mem_n @ wv).reshape(B, M, X_HEADS, X_HD)
    s = jnp.einsum('bthd,bmhd->bhtm', q, k).astype(jnp.float32) * (X_HD ** -0.5)
    p = jax.nn.softmax(s, axis=-1).astype(v.dtype)
    o = jnp.einsum('bhtm,bmhd->bthd', p, v).reshape(B, T, X_W)
    return o @ wo

def setup_inputs(seed: int = 0) -> dict:
    key = jax.random.key(seed)
    ks = jax.random.split(key, 24)
    f32 = jnp.float32

    def nrm(k, shape, fan_in):
        return jax.random.normal(k, shape, f32) * (fan_in ** -0.5)

    def gain(k, shape):
        return 1.0 + 0.05 * jax.random.normal(k, shape, f32)

    x = jax.random.normal(ks[0], (BATCH, SEQ, D_MODEL), f32)
    mem = jax.random.normal(ks[1], (BATCH, N_MEM, D_MODEL), f32)
    offset = jax.random.randint(ks[2], (BATCH, 1), 0, MAX_OFFSET, dtype=jnp.int32)
    positions = offset + jnp.arange(SEQ, dtype=jnp.int32)[None, :]
    return {
        'x': x,
        'mem': mem,
        'positions': positions,
        'norm_mix': gain(ks[3], (DEPTH, D_MODEL)),
        'w_in': nrm(ks[4], (DEPTH, D_MODEL, IN_W), D_MODEL),
        'hg_lower': 0.5 * jax.random.normal(ks[5], (DEPTH + 1, HG_KW), f32),
        'hg_norm': gain(ks[6], (DEPTH, HG_VW)),
        'sw_sinks': 0.5 * jax.random.normal(ks[7], (DEPTH, SW_HEADS), f32),
        'w_proj_a': nrm(ks[8], (DEPTH, HG_VW, D_MODEL), HG_VW),
        'w_proj_b': nrm(ks[9], (DEPTH, SW_QW, D_MODEL), SW_QW),
        'w_out': nrm(ks[10], (DEPTH, D_MODEL, D_MODEL), D_MODEL),
        'norm_x': gain(ks[11], (DEPTH, D_MODEL)),
        'norm_mem': gain(ks[12], (DEPTH, D_MODEL)),
        'wq_x': nrm(ks[13], (DEPTH, D_MODEL, X_W), D_MODEL),
        'wk_x': nrm(ks[14], (DEPTH, D_MODEL, X_W), D_MODEL),
        'wv_x': nrm(ks[15], (DEPTH, D_MODEL, X_W), D_MODEL),
        'wo_x': nrm(ks[16], (DEPTH, X_W, D_MODEL), X_W),
        'norm_ffn': gain(ks[17], (DEPTH, D_MODEL)),
        'w_gate': nrm(ks[18], (DEPTH, D_MODEL, D_FF), D_MODEL),
        'w_up': nrm(ks[19], (DEPTH, D_MODEL, D_FF), D_MODEL),
        'w_down': nrm(ks[20], (DEPTH, D_FF, D_MODEL), D_FF),
        'norm_final': gain(ks[21], (D_MODEL,)),
    }

def reference(x, mem, positions, norm_mix, w_in, hg_lower, hg_norm, sw_sinks, w_proj_a, w_proj_b,
              w_out, norm_x, norm_mem, wq_x, wk_x, wv_x, wo_x, norm_ffn, w_gate, w_up, w_down,
              norm_final):
    lb_table = jnp.cumsum(jax.nn.softmax(hg_lower.astype(jnp.float32), axis=0), axis=0)
    for l in range(DEPTH):
        h = rmsnorm(x, norm_mix[l])
        proj = h @ w_in[l]
        q_a, f_a, i_a, g_a, q_b, k_b, v_b, gate_a, gate_b = jnp.split(proj, IN_OFFSETS, axis=-1)
        o_a = hgrn2_mixer(q_a, f_a, i_a, g_a, lb_table[l], hg_norm[l])
        o_b = swa_mixer(q_b, k_b, v_b, positions, sw_sinks[l])
        y_a = o_a @ w_proj_a[l]
        y_b = o_b @ w_proj_b[l]
        merged = jax.nn.sigmoid(gate_a) * y_a + jax.nn.sigmoid(gate_b) * y_b
        x = x + merged @ w_out[l]
        hx = rmsnorm(x, norm_x[l])
        mem_n = rmsnorm(mem, norm_mem[l])
        x = x + cross_attn(hx, mem_n, wq_x[l], wk_x[l], wv_x[l], wo_x[l])
        hf = rmsnorm(x, norm_ffn[l])
        x = x + (jax.nn.silu(hf @ w_gate[l]) * (hf @ w_up[l])) @ w_down[l]
    return rmsnorm(x, norm_final)


_drawn_inputs = setup_inputs


def setup_inputs(seed=0):
    import zlib

    import numpy as np

    out = dict(_drawn_inputs(seed))
    spreads = {}
    factors = {'hg_norm': 3.181, 'sw_sinks': 8.0, 'norm_x': 8.0, 'norm_mem': 7.242, 'norm_ffn': 8.0}
    for name, (base, spread) in spreads.items():
        noise = np.random.default_rng([zlib.crc32(name.encode()), seed]).standard_normal(out[name].shape)
        drawn = base * np.exp(spread * noise) if base else spread * noise
        out[name] = __import__('jax').numpy.asarray(drawn.astype(out[name].dtype))
    for name, factor in factors.items():
        out[name] = (out[name] * factor).astype(out[name].dtype)
    return out
```

```python
from contextlib import ExitStack

import concourse.bass as bass
from concourse import mybir

P = 128
D = 2048
T = 512
M = 256
KT = D // P
TT = T // P
MT = M // P
EPS = 1e-6
HEADS = 8
BLK = 128
NB = T // BLK
LEVELS = [64, 32, 16, 8, 4, 2, 1]
NL = len(LEVELS)
SWH, SWKV, HD = 16, 4, 64
WIN = 128
XH = 4
DFF = 5632
FB = 4
NFB = DFF // (P * FB)
SW_SCALE = HD ** -0.5
X_SCALE = P ** -0.5
NEVER = -3.0e38

Q_A, F_A, I_A, G_A = 0, 1024, 2048, 3072
Q_B, K_B, V_B = 4096, 5120, 5376
GATE_A, GATE_B = 5632, 7680

CK = 8
RING = 4
LEAD = 2
C_K, C_V, C_H, C_GA, C_S, C_GB, C_O, C_XQ, C_XO, C_F = 0, 8, 16, 80, 128, 152, 200, 232, 240, 248
CF_BLOCK = 2 * 2 * FB + 8
C_END = C_F + NFB * CF_BLOCK

G_MIX, G_X, G_FFN, G_MEM, G_LB, G_HN, G_ROWS = 0, 16, 32, 48, 64, 80, 88

ALU = mybir.AluOpType
ACT = mybir.ActivationFunctionType
AX = mybir.AxisListType
F32 = mybir.dt.float32
F32R = mybir.dt.float32r
I32 = mybir.dt.int32
KB = 1024



def level_view(t, w):
    return t.rearrange("p (b s w) -> p b s w", s=2, w=w)


def build_trunk(nc, a, out):
    ctx = ExitStack()
    with ctx:
        base = (nc.sbuf_base + 63) // 64 * 64

        def at(name, off, shape, dt):
            return nc.alloc_sbuf_tensor_at(name, shape, dt, offset=base + int(off))

        sems = {}

        def S(name):
            if name not in sems:
                sems[name] = ctx.enter_context(nc.semaphore(name))
            return sems[name]

        op_hi = at("op_hi", 0, [P, KT, T], F32R)
        op_lo = at("op_lo", 32 * KB, [P, KT, T], F32R)
        x_nat = at("x_nat", 64 * KB, [P, TT, D], F32)
        res = at("res", 64 * KB, [P, KT, T], F32)
        a_hi = at("a_hi", 64 * KB, [P, FB, T], F32R)
        a_lo = at("a_lo", 72 * KB, [P, FB, T], F32R)
        mem_hi = at("mem_hi", 96 * KB, [P, KT, M], F32R)
        mem_lo = at("mem_lo", 112 * KB, [P, KT, M], F32R)
        o_hi = at("o_hi", 96 * KB, [P, HEADS, T], F32R)
        o_lo = at("o_lo", 112 * KB, [P, HEADS, T], F32R)
        x2_nat = at("x2_nat", 96 * KB, [P, TT, D], F32)
        w_raw = at("w_raw", 128 * KB, [P, RING, CK * P], F32)
        w_hi = at("w_hi", 144 * KB, [P, RING, CK * P], F32R)
        w_lo = at("w_lo", 160 * KB, [P, RING, CK * P], F32R)
        ident = at("ident", 176 * KB, [P, P], F32)
        ones = at("ones", 176.5 * KB, [P, P], F32)
        gain_rows = at("gain_rows", 177 * KB, [P, P], F32)
        gains = at("gains", 177.5 * KB, [P, G_ROWS], F32)
        stat = at("stat", 177.5 * KB + 384, [P, 32], F32)
        SCR = 178 * KB
        mem_nat = at("mem_nat", SCR, [P, MT, D], F32)
        kv_mem = at("kv_mem", SCR + 16 * KB, [P, 4, 512], F32)
        lb_t = at("lb_t", SCR + 29 * KB, [P, 5, HEADS], F32)
        HB = 64 * KB
        q_t = at("q_t", HB, [P, 2, T], F32)
        v_nat = at("v_nat", HB + 4 * KB, [P, 2, T], F32)
        silu_g = at("silu_g", HB + 8 * KB, [P, 2, T], F32)
        sig_f = at("sig_f", HB + 12 * KB, [P, T], F32)
        f_t = at("f_t", HB + 14 * KB, [P, T], F32)
        log_f = at("log_f_t", HB + 16 * KB, [P, T], F32)
        k_t = at("k_t", HB + 18 * KB, [P, T], F32)
        b_t = at("b_t", HB + 20 * KB, [P, T], F32)
        exp_b = at("exp_b_t", HB + 22 * KB, [P, T], F32)
        d_lev = at("d_lev", HB + 24 * KB, [P, 2, T], F32)
        qk_lev = at("qk_lev", HB + 28 * KB, [P, 2, T], F32)
        h_scr = SCR
        scores_a = at("scores_a", h_scr, [P, T], F32)
        qe_t = at("qe_t", h_scr + 2 * KB, [P, T], F32)
        kh_t = at("kh_t", h_scr + 4 * KB, [P, T], F32)
        kh_nat = at("kh_nat", h_scr + 6 * KB, [P, T], F32)
        vT_t = at("vT_t", h_scr + 8 * KB, [P, T], F32)
        osq_t = at("osq_t", h_scr + 10 * KB, [P, T], F32)
        orstd_t = at("orstd_t", h_scr + 12 * KB, [P, T], F32)
        o1_t = at("o1_t", h_scr + 14 * KB, [P, T], F32)
        o2_t = at("o2_t", h_scr + 16 * KB, [P, T], F32)
        state = at("state_t", h_scr + 18 * KB, [P, NB - 1, P], F32)
        sig_g = at("sig_g", h_scr + 19.5 * KB, [P, T], F32)
        scan_mask = at("scan_mask", h_scr + 21.5 * KB, [P, T], F32)
        masks = at("masks", h_scr + 23.5 * KB, [P, NL, P], I32)
        gate_t = at("gate_t", SCR + 25 * KB, [P, 2, T], F32)

        eps_col = stat[:, 31:32]
        cos_t = at("cos_t", SCR, [P, T], F32)
        sin_t = at("sin_t", SCR + 2 * KB, [P, T], F32)
        q_rot = at("q_rot", SCR + 4 * KB, [P, T], F32)
        swapped = at("swapped_t", SCR + 6 * KB, [P, T], F32)
        probs = at("probs_t", SCR + 8 * KB, [P, 2, 512], F32)
        probs_T = at("probs_T", SCR + 12 * KB, [P, 2, 512], F32)
        v_win = at("v_win", SCR + 16 * KB, [P, T // 64, HD], F32)
        kT_pad = at("kT_pad", SCR + 18 * KB, [P, 64 + T], F32)
        vT_pad = at("vT_pad", SCR + 18 * KB + 2304, [P, 64 + T], F32)
        sw_cols = at("sw_cols", SCR + 22.5 * KB, [P, 2, SWH], F32)
        sw_small = at("sw_small", SCR + 22.75 * KB, [P, 2, 5, TT], F32)
        rope_cols = at("rope_cols", SCR + 23 * KB, [P, 2], F32)
        angle = at("angle", SCR + 8 * KB, [P, T], F32)
        turns = at("turns", SCR + 10 * KB, [P, T], F32)
        pos_i = at("pos_i", SCR + 12 * KB, [P, T], I32)
        x_cols = at("x_cols", SCR, [P, 2, TT, P], F32)
        xT_buf = at("xT_buf", SCR + 4 * KB, [P, 2, T], F32)
        sq_t = at("sq_t", SCR + 8 * KB, [P, T], F32)
        sq_sum = at("sq_sum_t", SCR + 24 * KB, [P, T], F32)
        rstd_t = at("rstd_t", SCR + 26 * KB, [P, T], F32)
        v_t = at("v_t", SCR + 8 * KB, [P, T], F32)
        n_t = at("n_t", SCR + 10 * KB, [P, T], F32)
        kv_x = at("kv_x", SCR, [P, 4, 512], F32)
        q_x = at("q_x", SCR + 12 * KB, [P, XH, T], F32)
        p_x = at("p_x", SCR + 20 * KB, [P, TT, M], F32)
        pT_x = at("pT_x", SCR + 8 * KB, [P, MT, T], F32)
        x_small = at("x_small", SCR + 28 * KB, [P, 3, TT], F32)
        g1_t = at("g1_t", SCR, [P, T], F32)
        u1_t = at("u1_t", SCR + 2 * KB, [P, T], F32)
        sg_t = at("sg_t", SCR + 4 * KB, [P, T], F32)
        a_t = at("a_t", SCR + 6 * KB, [P, T], F32)
        g_final = at("g_final", SCR + 14 * KB, [P, D], F32)
        junk = at("junk", SCR + 12 * KB, [P, 512], F32)
        f_stat = at("f_stat", SCR + 28 * KB, [P, 8, TT], F32)

        psum = ctx.enter_context(nc.psum_tensor("psum", [P, 8, 512], F32))
        bank = [psum[:, i] for i in range(8)]

        w_loaded = [S(f"w_loaded{i}") for i in range(RING)]
        w_hi_ready, w_lo_ready = S("w_hi_ready"), S("w_lo_ready")
        chunk_done = S("chunk_done")

        mem_kv_dram = nc.dram_tensor("mem_kv_scratch", [P, 4, 512], F32, kind="Internal").ap()
        xT_dram = nc.dram_tensor("xT_scratch", [KT, P, T], F32, kind="Internal").ap()

        block = ctx.enter_context(nc.Block())

        def before(eng, semaphore, count, v=0, k=0):
            if isinstance(v, int):
                count, v = count + v * k, 0
                if count > 0:
                    eng.wait_ge(semaphore, count)
            else:
                eng.wait_ge(semaphore, v * k + count)

        def cols(w, c0, width, k0=0, nk=CK):
            v = w.rearrange("(k p) n -> p k n", p=P)[:, k0:k0 + nk]
            return v[:, :, bass.ds(c0, width)]

        w_in = a["w_in"].rearrange("l d n -> (l d) n")

        @block.sync
        def _(sp):
            def load(src, s, v=0, k=0, shape="p (k n) -> p k n", **size):
                before(sp, w_lo_ready, s - RING + 1, v, k)
                if not isinstance(v, int):
                    sp.sem_inc(S("slot_free"), 1)
                dst = w_raw[:, s % RING].rearrange(shape, **size)
                sp.dma_start(dst, src).then_inc(w_loaded[s % RING], 16)

            def unit(w, c0, s, v=0, k=0, chunks=2):
                for j in range(chunks):
                    load(cols(w, c0, P, j * CK), s + j, v, k, n=P)

            sp.dma_start(gain_rows[0:16, :], a["norm_mix"].rearrange("l (k p) -> (l k) p", p=P)).then_inc(S("const_in"), 16)
            sp.dma_start(gain_rows[16:32, :], a["norm_x"].rearrange("l (k p) -> (l k) p", p=P)).then_inc(S("const_in"), 16)
            sp.dma_start(gain_rows[32:48, :], a["norm_ffn"].rearrange("l (k p) -> (l k) p", p=P)).then_inc(S("const_in"), 16)
            sp.dma_start(gain_rows[48:64, :], a["norm_mem"].rearrange("l (k p) -> (l k) p", p=P)).then_inc(S("const_in"), 16)
            sp.dma_start(gain_rows[64:80, :], a["hg_lower"].rearrange("l (k p) -> (l k) p", p=P)).then_inc(S("const_in"), 16)
            sp.dma_start(gain_rows[80:88, :], a["hg_norm"].rearrange("l (k p) -> (l k) p", p=P)).then_inc(S("const_in"), 16)
            sp.dma_start(ident[:, :], a["consts"][:, 0:P]).then_inc(S("const_in"), 16)
            for t in range(MT):
                sp.dma_start(mem_nat[:, t], a["mem"][0, t * P:(t + 1) * P, :]).then_inc(S(f"nat_in{t}"), 16)
            wk = a["wk_x"].rearrange("l d n -> (l d) n")
            wv = a["wv_x"].rearrange("l d n -> (l d) n").rearrange("(k p) n -> p k n", p=P)
            for s in range(RING):
                load(cols(wk, s // 2 * P, P, s % 2 * CK), C_K + s, n=P)
            for t in range(TT):
                sp.dma_start(x_nat[:, t], a["x"][0, t * P:(t + 1) * P, :]).then_inc(S(f"nat_in{MT + t}"), 16)
            for s in range(RING, 8):
                load(cols(wk, s // 2 * P, P, s % 2 * CK), C_K + s, n=P)
            for s in range(8):
                load(wv[:, 2 * s:2 * s + 2], C_V + s, n=512)
            for s in range(RING):
                load(cols(w_in, (Q_A, I_A)[s // 2], P, s % 2 * CK), C_H + s, n=P)
            for j in range(4):
                sp.wait_ge(S("kv_copied"), 4 + 2)
                sp.dma_start(mem_kv_dram[:, j], kv_mem[:, j]).then_inc(S("kv_stored"), 16)
            sp.wait_ge(S("kv_stored"), 64)
            sp.dma_start(scan_mask[:, :], a["consts"][:, P:P + T]).then_inc(S("h_const_in"), 16)
            sp.dma_start(masks[:, :, :], a["masks"]).then_inc(S("h_const_in"), 16)

            def head_loads(h, s0, v, k):
                for j, c0 in enumerate((Q_A, I_A, F_A, G_A)):
                    if isinstance(h, int) and h == 0 and j < 2:
                        continue
                    unit(w_in, h * P + c0, s0 + 2 * j, v, k)

            for h in range(2):
                head_loads(h, C_H + 8 * h, 0, 0)
            with sp.Fori(0, 3) as i:
                for x in range(2):
                    head_loads(i * 2 + (2 + x), C_H + 16 + 8 * x, i, 16)

            def gate_loads(gate0, w_proj, s0):
                with sp.Fori(0, 4) as i:
                    for x in range(4):
                        m0 = i * (4 * P) + x * P
                        unit(w_in, m0 + gate0, s0 + 3 * x, i, 12)
                        unit(w_proj, m0, s0 + 3 * x + 2, i, 12, chunks=1)

            gate_loads(GATE_A, a["w_proj_a"].rearrange("l d n -> (l d) n"), C_GA)
            sp.wait_ge(S("o_split"), HEADS)
            sp.dma_start(pos_i[:, :], a["positions"].partition_broadcast(P).rearrange("p b t -> p (b t)")).then_inc(S("sw_in"), 16)
            sp.dma_start(sw_cols[:, 0, :], a["sw_sinks"].partition_broadcast(P).rearrange("p l h -> p (l h)")).then_inc(S("sw_in"), 16)
            sp.dma_start(rope_cols[:, :], a["consts"][:, P + T:P + T + 2]).then_inc(S("sw_in"), 16)
            for g in range(SWKV):
                s = C_S + 6 * g
                for j in range(2):
                    before(sp, w_lo_ready, s + j - RING + 1)
                    dst = w_raw[:, (s + j) % RING].rearrange("p (k n) -> p k n", n=P)
                    sp.dma_start(dst[:, :, HD:P], cols(w_in, V_B + g * HD, HD, j * CK)).then_inc(S("v_cols_in"), 16)
                    sp.wait_ge(S("v_cols_in"), 16 * (2 * g + j + 1))
                    sp.dma_start(dst[:, :, 0:HD], cols(w_in, K_B + g * HD, HD, j * CK)).then_inc(w_loaded[(s + j) % RING], 16)
                for x in range(2):
                    unit(w_in, Q_B + (2 * g + x) * P, s + 2 + 2 * x)
            gate_loads(GATE_B, a["w_proj_b"].rearrange("l d n -> (l d) n"), C_GB)
            w_out = a["w_out"].rearrange("l d n -> (l d) n")
            x_blocks = a["x"].rearrange("b (t p) d -> p (b t) d", p=P)
            sp.wait_ge(S("o_split"), 2 * HEADS)
            with sp.Fori(0, 8) as i:
                for x in range(2):
                    sp.wait_ge(S("xT_copied"), i * 2 + (x + 1))
                    sp.sem_inc(S("slot_free"), 1)
                    sp.dma_start(x_cols[:, x], x_blocks[:, :, bass.ds(i * (2 * P) + x * P, P)]).then_inc(S(f"x_cols_in{x}"), 16)
                    unit(w_out, i * (2 * P) + x * P, C_O + 2 * x, i, 4)
            wq = a["wq_x"].rearrange("l d n -> (l d) n")
            for u in range(XH):
                unit(wq, u * P, C_XQ + 2 * u)
            wo = a["wo_x"].rearrange("l (k p) n -> p (l k) n", p=P)
            for s in range(8):
                if s == 4:
                    sp.wait_ge(S("x1_ready"), KT + 2)
                    sp.wait_ge(S("rstd_x"), 1)
                    sp.dma_start(kv_x[:, :, :], mem_kv_dram[:, :, :]).then_inc(S("kv_in"), 16)
                load(wo[:, :, s * M:(s + 1) * M], C_XO + s, n=M)
            w_gate = a["w_gate"].rearrange("l d n -> (l d) n")
            w_up = a["w_up"].rearrange("l d n -> (l d) n")
            w_down = a["w_down"].rearrange("l (k p) n -> p (l k) n", p=P)

            def block_loads(b, v, k):
                for f in range(FB):
                    c0 = b * (FB * P) + f * P
                    unit(w_gate, c0, C_F + 4 * f, v, k)
                    unit(w_up, c0, C_F + 4 * f + 2, v, k)
                for d in range(4):
                    for j in range(2):
                        load(w_down[:, bass.ds(b * FB + 2 * j, 2), d * 512:(d + 1) * 512],
                             C_F + 16 + 2 * d + j, v, k, n=512)

            with sp.Fori(0, NFB) as b:
                block_loads(b, b, CF_BLOCK)
            sp.wait_ge(S("q_scaled"), XH)
            sp.dma_start(g_final[:, :], a["norm_final"].partition_broadcast(P)).then_inc(S("g_final_in"), 16)
            for t in range(TT):
                sp.wait_ge(S("out_ready"), t + 1)
                sp.dma_start(out[0, t * P:(t + 1) * P, :], x2_nat[:, t]).then_inc(S("stored"), 16)
            sp.wait_ge(S("stored"), 16 * TT)

        @block.gpsimd
        def _(pool):
            pool.memset(ones[:, :], 1.0).then_inc(S("ones_set"), 1)

            def split_lo(s, v=0, k=0):
                slot = s % RING
                before(pool, w_hi_ready, s + 1, v, k)
                before(pool, chunk_done, s - RING + 1, v, k)
                pool.tensor_tensor(w_lo[:, slot], w_raw[:, slot], w_hi[:, slot].bitcast(F32),
                                   ALU.subtract).then_inc(w_lo_ready, 1)

            for s in range(RING):
                split_lo(s)
            with pool.Fori(1, C_END // RING) as i:
                for s in range(RING):
                    split_lo(s, i, RING)

        @block.tensor
        def _(pe):
            def products(b, n, whl, xhl, start, stop):
                (wh, wl), (xh, xl) = whl, xhl
                pe.matmul(b[:, 0:n], wl, xh, start=start, stop=False)
                pe.matmul(b[:, 0:n], wh, xl, start=False, stop=False)
                return pe.matmul(b[:, 0:n], wh, xh, start=False, stop=stop)

            def chunk(b, s, v, k, hi, lo, k0, nk, n=T, split_base=None):
                before(pe, w_lo_ready, s + 1, v, k)
                slot = s % RING
                for j in range(CK):
                    kt = k0 + j
                    if split_base is not None:
                        pe.wait_ge(S("op_ready"), split_base + kt + 1)
                    w = [t[:, slot, j * P:(j + 1) * P] for t in (w_hi, w_lo)]
                    last = products(b, n, w, (hi[:, kt, :], lo[:, kt, :]), kt == 0, kt == nk - 1)
                last.then_inc(chunk_done, 1)

            pe.wait_ge(S("const_in"), 7 * 16)
            pe.transpose(bank[0][:, 0:G_ROWS], gain_rows[0:G_ROWS, :], ident[0:G_ROWS, 0:G_ROWS]).then_inc(S("gains_turned"), 1)
            pe.wait_ge(S("nat_scaled"), MT)
            for kt in range(KT):
                if kt >= 2:
                    pe.wait_ge(S("op_ready"), kt - 1)
                for t in range(MT):
                    last = pe.transpose(bank[2 + kt % 2][:, t * P:(t + 1) * P], mem_nat[:, t, kt * P:(kt + 1) * P], ident[:, :])
                last.then_inc(S("turned"), 1)
            pe.wait_ge(S("gains_ready"), 1)
            for u in range(XH):
                if u >= 2:
                    pe.wait_ge(S("kv_copied"), u - 1)
                for j in range(2):
                    chunk(bank[u % 2], C_K + 2 * u + j, 0, 0, mem_hi, mem_lo, j * CK, KT, n=M,
                          split_base=0 if u == 0 else None)
            pe.wait_ge(S("kv_copied"), 4)
            for q in range(8):
                before(pe, w_lo_ready, C_V + q + 1)
                slot = (C_V + q) % RING
                for j in range(2):
                    kt = 2 * q + j
                    for t in range(MT):
                        w = [x[:, slot, j * 512:(j + 1) * 512] for x in (w_hi, w_lo)]
                        m = [x[:, kt, t * P:(t + 1) * P] for x in (mem_hi, mem_lo)]
                        last = products(bank[t], 512, m, w, kt == 0, kt == KT - 1)
                last.then_inc(chunk_done, 1)
            for kt in range(KT):
                for t in range(TT):
                    if kt == 0:
                        pe.wait_ge(S("nat_scaled"), MT + t + 1)
                    if t == 0:
                        pe.wait_ge(S("op_ready"), KT + kt - 1)
                    last = pe.transpose(bank[2 + kt % 2][:, t * P:(t + 1) * P], x_nat[:, t, kt * P:(kt + 1) * P], ident[:, :])
                last.then_inc(S("turned"), 1)

            def head(h, par, project=True, mix=True, tail=True, first=False, s0=C_H, v=0, k=0):
                p, old = h - 1, 1 - par

                def level(l):
                    b = bank[2 + l % 2]
                    if l == 0:
                        pe.wait_ge(S("q_copied"), p + 1)
                        pe.wait_ge(S("k_ready"), p + 1)
                    else:
                        pe.wait_ge(S("qk_level"), p * NL + l)
                    before(pe, S("level_taken"), l - 1, p, NL + 1)
                    for c in range(NB):
                        f = slice(c * BLK, (c + 1) * BLK)
                        w, x = (k_t[:, f], q_t[:, old, f]) if l == 0 else (qk_lev[:, l % 2, f],) * 2
                        last = pe.matmul(b[:, f], w, x, start=True, stop=True)
                    last.then_inc(S("level_done"), 1)

                for c in range(CK):
                    if c == 1 and tail:
                        pe.wait_ge(S("o_squared"), h - 1)
                        pe.wait_ge(S("kh_nat_ready"), h - 1)
                        pe.matmul(bank[5], ones[:, :], osq_t[:, :], start=True, stop=True).then_inc(S("mean_done"), 1)
                    if mix and 2 <= c < 6:
                        level(2 * (c - 2))
                        level(2 * (c - 2) + 1)
                    if mix and c == 5:
                        pe.wait_ge(S("khat_ready"), p + 1)
                        before(pe, S("ln_mean"), 0, p, 1)
                        for x in range(NB):
                            f = slice(x * BLK, (x + 1) * BLK)
                            last = pe.transpose(bank[5][:, f], kh_t[:, f], ident[:, :])
                        last.then_inc(S("kh_turned"), 1)
                    if mix and c == 6:
                        pe.wait_ge(S("kh_nat_ready"), p + 1)
                        pe.wait_ge(S("v_nat_ready"), p + 1)
                        before(pe, S("state_ready"), 0, p, NB - 1)
                        for x in range(NB - 1):
                            f = slice(x * BLK, (x + 1) * BLK)
                            last = pe.matmul(bank[7][:, f], kh_nat[:, f], v_nat[:, old, f], start=True, stop=True)
                        last.then_inc(S("ds_done"), 1)
                    if mix and c == 7:
                        pe.wait_ge(S("level_taken"), (p + 1) * (NL + 1))
                        pe.wait_ge(S("state_ready"), (p + 1) * (NB - 1))
                        pe.wait_ge(S("qe_ready"), p + 1)
                        before(pe, S("o_scaled"), 0, p, 1)
                        for x in range(NB):
                            f = slice(x * BLK, (x + 1) * BLK)
                            last = pe.matmul(bank[6][:, f], v_nat[:, old, f], scores_a[:, f], start=True, stop=x == 0)
                            if x:
                                last = pe.matmul(bank[6][:, f], state[:, x - 1, :], qe_t[:, f], start=False, stop=True)
                        last.then_inc(S("o_done"), 1)
                    if project and c == 6:
                        pe.wait_ge(S("vT_copied"), h + 1)
                        before(pe, S("v_nat_ready"), 0, h, 1)
                        for x in range(NB):
                            f = slice(x * BLK, (x + 1) * BLK)
                            last = pe.transpose(bank[4][:, f], vT_t[:, f], ident[:, :])
                        last.then_inc(S("v_turned"), 1)
                    if project:
                        if c == 0:
                            before(pe, S("f_sig"), 0, h, 1)
                        if c == 2:
                            before(pe, S("silu_ready"), 0, h, 1)
                        if c == 4:
                            pe.wait_ge(S("q_copied"), h + 1)
                        if c == 6:
                            pe.wait_ge(S("vT_copied"), h + 1)
                        chunk(bank[c // 2 % 2], s0 + c, v, k, op_hi, op_lo, c % 2 * CK, KT,
                              split_base=KT if first and c < 2 else None)

            pe.wait_ge(S("kv_copied"), XH + MT)
            head(0, 0, mix=False, tail=False, first=True)
            head(1, 1, tail=False, s0=C_H + 8)
            with pe.Fori(0, 3) as i:
                for x in range(2):
                    head(i * 2 + (2 + x), x, s0=C_H + 16 + 8 * x, v=i, k=16)
            head(8, 0, project=False)
            head(9, 1, project=False, mix=False)
            pe.wait_ge(S("f_sig"), HEADS)
            pe.wait_ge(S("silu_ready"), HEADS)

            def gate_stage(s0, m0, o_count):
                with pe.Fori(0, 4) as i:
                    for x in range(4):
                        before(pe, S("gate_sig"), m0 + x + 1, i, 4)
                        for j in range(2):
                            chunk(bank[0], s0 + 3 * x + j, i, 12, op_hi, op_lo, j * CK, KT)
                        pe.wait_ge(S("o_split"), o_count)
                        before(pe, S("y_gated"), m0 + x + 2, i, 4)
                        chunk(bank[1], s0 + 3 * x + 2, i, 12, o_hi, o_lo, 0, CK)

            gate_stage(C_GA, 0, HEADS)

            def sw_scores(j):
                pe.wait_ge(S("q_roped"), j + 1)
                pe.wait_ge(S("k_roped"), j // 2 + 1)
                before(pe, S("probs_done"), 2 * j)
                for x in range(2):
                    r = slice(64 * x, 64 * x + 64)
                    for n in range(T // 64):
                        o = bank[2 + x][64 * (n % 2):64 * (n % 2) + 64, n // 2 * WIN:(n // 2 + 1) * WIN]
                        last = pe.matmul(o, q_rot[r, 64 * n:64 * n + 64], kT_pad[r, 64 * n:64 * n + WIN], start=True, stop=True)
                last.then_inc(S("scores_done"), 1)

            def sw_turn(j):
                pe.wait_ge(S("probs_ready"), 2 * (j + 1))
                before(pe, S("probs_T_ready"), 2 * j)
                for x in range(2):
                    for t in range(TT):
                        f = slice(t * P, (t + 1) * P)
                        last = pe.transpose(bank[5 + 2 * x][:, f], probs[:, x, f], ident[:, :])
                last.then_inc(S("probs_turned"), 1)

            def sw_values(j):
                pe.wait_ge(S("probs_T_ready"), 2 * (j + 1))
                pe.wait_ge(S("v_win_ready"), j // 2 + 1)
                before(pe, S("o_split"), HEADS + j)
                for x in range(2):
                    for n in range(T // 64):
                        f = slice(64 * n, 64 * n + 64)
                        last = pe.matmul(bank[6][64 * x:64 * x + 64, f], v_win[:, n, :], probs_T[:, x, f], start=True, stop=True)
                last.then_inc(S("sw_o_done"), 1)

            def sw_windows(g):
                pe.wait_ge(S("vT_padded"), g + 1)
                before(pe, S("v_win_ready"), g)
                for n in range(T // 64):
                    last = pe.transpose(bank[4][:, HD * n:HD * (n + 1)], vT_pad[64:128, 64 * n:64 * n + WIN], ident[64:128, 64:128])
                last.then_inc(S("windows_turned"), 1)

            tile_of = {3 * g + 1 + x: 2 * g + x for g in range(SWKV) for x in range(2)}
            for n in range(3 * SWKV + 2):
                if n - 2 in tile_of:
                    sw_turn(tile_of[n - 2])
                if n < 3 * SWKV:
                    if n < 2:
                        pe.wait_ge(S("y_gated"), KT + 2) if n else pe.wait_ge(S("gate_sig"), KT + 1)
                    else:
                        pe.wait_ge(S("rope_mul"), n - 1)
                    chunk(bank[n % 2], C_S + 2 * n, 0, 0, op_hi, op_lo, 0, KT)
                if n - 1 in tile_of:
                    sw_scores(tile_of[n - 1])
                if n - 2 in tile_of:
                    sw_values(tile_of[n - 2])
                if n % 3 == 1 and n < 3 * SWKV:
                    sw_windows(n // 3)
                if n < 3 * SWKV:
                    chunk(bank[n % 2], C_S + 2 * n + 1, 0, 0, op_hi, op_lo, CK, KT)
            pe.wait_ge(S("rope_mul"), 3 * SWKV)
            gate_stage(C_GB, KT, 2 * HEADS)

            with pe.Fori(0, 8) as i:
                for x in range(2):
                    pe.wait_ge(S(f"x_cols_in{x}"), i * 16 + 16)
                    pe.wait_ge(S("x1_ready"), i * 2 + (x + 1))
                    for t in range(TT):
                        last = pe.transpose(bank[4 + x][:, t * P:(t + 1) * P], x_cols[:, x, t, :], ident[:, :])
                    last.then_inc(S("xT_turned"), 1)
                    for j in range(2):
                        chunk(bank[x], C_O + 2 * x + j, i, 4, op_hi, op_lo, j * CK, KT,
                              split_base=2 * KT if x == 0 else None)

            def mean_square(n, count):
                pe.wait_ge(S("sq_summed"), count)
                pe.matmul(bank[6], ones[:, :], sq_sum[:, :], start=True, stop=True).then_inc(S("x_mean_done"), 1)

            for u in range(XH):
                if u >= 2:
                    pe.wait_ge(S("q_scaled"), u - 1)
                else:
                    pe.wait_ge(S("x1_ready"), KT + 2)
                for j in range(2):
                    chunk(bank[u % 2], C_XQ + 2 * u + j, 0, 0, op_hi, op_lo, j * CK, KT,
                          split_base=3 * KT if u == 0 else None)
                if u == 0:
                    mean_square(0, KT)
            pe.wait_ge(S("kv_in"), 16)

            def x_scores(h):
                pe.wait_ge(S("q_scaled"), h + 1)
                if h:
                    pe.wait_ge(S("x_probs_done"), h)
                for t in range(TT):
                    o = psum[:, 2 + t // 2, (t % 2) * M:(t % 2 + 1) * M]
                    last = pe.matmul(o, q_x[:, h, t * P:(t + 1) * P], kv_x[:, h // 2, (h % 2) * M:(h % 2 + 1) * M], start=True, stop=True)
                last.then_inc(S("x_scores_done"), 1)

            x_scores(0)
            for h in range(XH):
                pe.wait_ge(S("x_probs_ready"), h + 1)
                if h:
                    pe.wait_ge(S("x_probs_T"), h)
                for m in range(MT):
                    for t in range(TT):
                        last = pe.transpose(bank[4 + m][:, t * P:(t + 1) * P], p_x[:, t, m * P:(m + 1) * P], ident[:, :])
                last.then_inc(S("x_turned"), 1)
                if h + 1 < XH:
                    x_scores(h + 1)
                pe.wait_ge(S("x_probs_T"), h + 1)
                if h:
                    pe.wait_ge(S("o_split"), 2 * HEADS + h)
                for m in range(MT):
                    last = pe.matmul(bank[7], kv_x[:, 2 + m, h * P:(h + 1) * P], pT_x[:, m, :], start=m == 0, stop=m == MT - 1)
                last.then_inc(S("x_o_done"), 1)
            with pe.Fori(0, 2) as i:
                for x in range(RING):
                    before(pe, w_lo_ready, C_XO + x + 1, i, 4)
                    pe.wait_ge(S("x2_ready"), i * 8 + (2 * x + 2))
                    for j in range(2):
                        b = bank[x % 2 * 2 + j]
                        for kt in range(XH):
                            pe.wait_ge(S("o_split"), 2 * HEADS + kt + 1)
                            f = slice(kt * M + j * P, kt * M + (j + 1) * P)
                            last = products(b, T, (w_hi[:, x, f], w_lo[:, x, f]), (o_hi[:, kt, :], o_lo[:, kt, :]), kt == 0, kt == XH - 1)
                    last.then_inc(chunk_done, 1)

            pe.wait_ge(S("x2_ready"), KT + 4)
            for kt in range(KT):
                if kt >= 2:
                    pe.wait_ge(S("x2_nat_ready"), kt - 1)
                for t in range(TT):
                    last = pe.transpose(bank[4 + kt % 2][:, t * P:(t + 1) * P], res[:, kt, t * P:(t + 1) * P], ident[:, :])
                last.then_inc(S("x2_turned"), 1)
            mean_square(1, 2 * KT)

            def ffn_block(v, k):
                for f in range(FB):
                    for u, name in enumerate(("gate_scaled", "up_scaled")):
                        if f:
                            before(pe, S(name), f, v, FB)
                        for j in range(2):
                            chunk(bank[u], C_F + 4 * f + 2 * u + j, v, k, op_hi, op_lo, j * CK, KT,
                                  split_base=4 * KT if f == u == 0 else None)
                for d in range(4):
                    banks = (2, 3, 4, 5) if d % 2 == 0 else (0, 1, 6, 7)
                    if d == 0:
                        pe.wait_ge(S("x2_nat_ready"), KT)
                    if d == 1:
                        before(pe, S("up_scaled"), FB, v, FB)
                    if d >= 2:
                        before(pe, S("down_added"), 4 * (d - 1), v, 16)
                    for j in range(2):
                        before(pe, w_lo_ready, C_F + 16 + 2 * d + j + 1, v, k)
                        slot = (2 * d + j) % RING
                        for x in range(2):
                            kt = 2 * j + x
                            if d == 0:
                                before(pe, S("a_split"), kt + 1, v, FB)
                            w = [y[:, slot, x * 512:(x + 1) * 512] for y in (w_hi, w_lo)]
                            for t in range(TT):
                                m = [y[:, kt, t * P:(t + 1) * P] for y in (a_hi, a_lo)]
                                last = products(bank[banks[t]], 512, m, w, kt == 0, kt == FB - 1)
                        last.then_inc(chunk_done, 1)
                before(pe, S("down_added"), 14, v, 16)

            with pe.Fori(0, NFB) as b:
                ffn_block(b, CF_BLOCK)

        @block.scalar
        def _(act):
            def split_hi(s, v=0, k=0):
                slot = s % RING
                before(act, w_loaded[slot], 16 * (s // RING + 1), v, 16 * k // RING)
                before(act, chunk_done, s - RING + 1, v, k)
                act.activation(w_hi[:, slot], w_raw[:, slot], ACT.Copy).then_inc(w_hi_ready, 1)

            def done(s, v=0, k=0):
                before(act, chunk_done, s + 1, v, k)

            act.sem_inc(S("gate_sig"), 1)
            act.sem_inc(S("xT_copied"), 2)

            def nat_stats(n):
                src = mem_nat[:, n] if n < MT else x_nat[:, n - MT]
                act.wait_ge(S(f"nat_in{n}"), 16)
                if n >= 1:
                    act.wait_ge(S("squared"), n)
                act.activation(psum[:, 4:8].rearrange("p b n -> p (b n)"), src, ACT.Square, accum_out=stat[:, n:n + 1]).then_inc(S("squared"), 1)
                act.wait_ge(S("mean_sq"), n + 1)
                act.activation(stat[:, 8 + n:9 + n], stat[:, 16 + n:17 + n], ACT.Ln).then_inc(S("ln_stat"), 1)
                act.wait_ge(S("ln_stat"), n + 1)
                act.activation(stat[:, 24 + n:25 + n], stat[:, 8 + n:9 + n], ACT.Exp, scale=-0.5).then_inc(S("rstd_stat"), 1)

            for n in range(MT):
                nat_stats(n)
            act.wait_ge(S("gains_turned"), 1)
            act.activation(gains[:, :], bank[0][:, 0:G_ROWS], ACT.Copy).then_inc(S("gains_ready"), 1)
            act.wait_ge(S("lb_shifted"), 1)
            act.activation(lb_t[:, 3:5], lb_t[:, 1:3], ACT.Exp).then_inc(S("lb_exp"), 1)
            for s in range(LEAD):
                split_hi(s)

            def turn_hi(g):
                kt = g % KT
                act.wait_ge(S("turned"), g + 1)
                if g < KT:
                    dst, n, gain = mem_hi, M, G_MEM
                else:
                    dst, n, gain = op_hi, T, G_MIX
                act.activation(dst[:, kt, :], bank[2 + kt % 2][:, 0:n], ACT.Copy, scale=gains[:, gain + kt:gain + kt + 1]).then_inc(S("op_hi_ready"), 1)

            act.wait_ge(S("gains_ready"), 1)
            for g in range(KT):
                turn_hi(g)
            for u in range(XH):
                for j in range(2):
                    split_hi(C_K + 2 * u + j + LEAD)
                nat_stats(MT + u)
                done(C_K + 2 * u + 1)
                act.activation(kv_mem[:, u // 2, (u % 2) * M:(u % 2 + 1) * M], bank[u % 2][:, 0:M], ACT.Copy).then_inc(S("kv_copied"), 1)
            for q in range(8):
                split_hi(C_V + q + LEAD)
            done(C_V + 7)
            for t in range(MT):
                act.activation(kv_mem[:, 2 + t], bank[t], ACT.Copy).then_inc(S("kv_copied"), 1)
            for g in range(KT, 2 * KT):
                turn_hi(g)
            act.wait_ge(S("kv_stored"), 64)
            act.wait_ge(S("h_const_in"), 32)

            def head(h, par, project=True, mix=True, tail=True, s0=C_H, v=0, k=0):
                p, old = h - 1, 1 - par

                def exp_level(l):
                    act.wait_ge(S("d_level"), p * NL + l)
                    act.activation(d_lev[:, l % 2], d_lev[:, l % 2], ACT.Exp).then_inc(S("exp_level"), 1)

                for c in range(CK):
                    if project:
                        split_hi(s0 + c + LEAD, v, k)
                    if c == 0 and mix:
                        act.wait_ge(S("f_ready"), p + 1)
                        act.activation(log_f[:, :], f_t[:, :], ACT.Ln).then_inc(S("log_f"), 1)
                    if c == 0 and tail:
                        act.wait_ge(S("o_done"), h - 1)
                        act.activation(osq_t[:, :], bank[6], ACT.Square).then_inc(S("o_squared"), 1)
                    if c == 1 and mix:
                        act.wait_ge(S("b_ready"), p + 1)
                        before(act, S("o_done"), 0, p, 1)
                        act.activation(exp_b[:, :], b_t[:, :], ACT.Exp).then_inc(S("exp_b"), 1)
                        exp_level(1)
                        exp_level(2)
                    if c == 2 and project:
                        done(s0 + 1, v, k)
                        act.activation(q_t[:, par], bank[0], ACT.Copy).then_inc(S("q_copied"), 1)
                    if c == 2 and tail:
                        act.wait_ge(S("mean_done"), h - 1)
                        before(act, S("o_scaled"), 0, h - 2, 1)
                        act.activation(orstd_t[:, :], bank[5], ACT.Ln, scale=1.0 / P, bias=eps_col[:, :]).then_inc(S("ln_mean"), 1)
                        act.wait_ge(S("ln_mean"), h - 1)
                        act.activation(orstd_t[:, :], orstd_t[:, :], ACT.Exp, scale=-0.5).then_inc(S("o_rstd"), 1)
                    if c == 2 and mix:
                        exp_level(3)
                        exp_level(4)
                    if c == 3 and mix:
                        exp_level(5)
                        exp_level(6)
                        exp_level(7)
                    if c == 3 and tail:
                        act.wait_ge(S("o_gated"), h - 1)
                        act.activation(o_hi[:, bass.ds(h - 2, 1), :], o2_t[:, None, :], ACT.Copy).then_inc(S("o_hi_ready"), 1)
                    if c == 4 and project:
                        done(s0 + 3, v, k)
                        before(act, S("v_turned"), 0, h, 1)
                        act.activation(vT_t[:, :], bank[1], ACT.Copy).then_inc(S("vT_copied"), 1)
                    if c == 4 and mix:
                        act.wait_ge(S("dk_ready"), p + 1)
                        act.activation(kh_t[:, :], kh_t[:, :], ACT.Exp).then_inc(S("exp_khat"), 1)
                    if c == 5 and mix:
                        act.wait_ge(S("kh_turned"), p + 1)
                        before(act, S("ds_done"), 0, p, 1)
                        act.activation(kh_nat[:, :], bank[5], ACT.Copy).then_inc(S("kh_nat_ready"), 1)
                    if c == 6 and project:
                        done(s0 + 5, v, k)
                        before(act, S("f_ready"), 0, h, 1)
                        act.activation(sig_f[:, :], bank[0], ACT.Sigmoid).then_inc(S("f_sig"), 1)
                if project:
                    done(s0 + 7, v, k)
                    before(act, S("silu_ready"), 0, h, 1)
                    act.activation(sig_g[:, :], bank[1], ACT.Sigmoid).then_inc(S("g_sig"), 1)

            head(0, 0, mix=False, tail=False)
            head(1, 1, tail=False, s0=C_H + 8)
            with act.Fori(0, 3) as i:
                for x in range(2):
                    head(i * 2 + (2 + x), x, s0=C_H + 16 + 8 * x, v=i, k=16)
            head(8, 0, project=False)
            head(9, 1, project=False, mix=False)

            def gate_stage(s0, m0):
                with act.Fori(0, 4) as i:
                    for x in range(4):
                        for j in range(3):
                            split_hi(s0 + 3 * x + j + LEAD, i, 12)
                        done(s0 + 3 * x + 1, i, 12)
                        before(act, S("y_gated"), m0 + x + 1, i, 4)
                        act.activation(gate_t[:, x % 2], bank[0], ACT.Sigmoid).then_inc(S("gate_sig"), 1)

            gate_stage(C_GA, 0)

            for n in range(2):
                act.wait_ge(S("angle_ready"), n + 1)
                act.activation((sin_t, cos_t)[n][:, :], turns[:, :], ACT.Sin).then_inc(S("sine"), 1)

            def sw_exps(j):
                for x in range(2):
                    h = 2 * j + x
                    act.wait_ge(S("sw_max"), h + 1)
                    before(act, S("probs_turned"), j)
                    for t in range(TT):
                        f = slice(t * P, (t + 1) * P)
                        act.activation(probs[:, x, f], bank[2 + x][:, f], ACT.Exp, scale=SW_SCALE,
                                       bias=sw_small[:, x, 0, t:t + 1], accum_out=sw_small[:, x, 1, t:t + 1])
                    act.activation(sw_small[:, x, 2, :], sw_small[:, x, 0, :], ACT.Exp, bias=sw_cols[:, 0, h:h + 1]).then_inc(S("probs_done"), 1)

            tile_of = {3 * g + 1 + x: 2 * g + x for g in range(SWKV) for x in range(2)}
            for n in range(3 * SWKV + 2):
                if n < 3 * SWKV:
                    split_hi(C_S + 2 * n + LEAD)
                if n - 2 in tile_of:
                    j = tile_of[n - 2]
                    act.wait_ge(S("probs_turned"), j + 1)
                    before(act, S("sw_o_done"), j)
                    act.activation(probs_T[:, 0], bank[5], ACT.Copy).then_inc(S("probs_T_ready"), 1)
                if n < 3 * SWKV:
                    split_hi(C_S + 2 * n + 1 + LEAD)
                if n - 1 in tile_of:
                    sw_exps(tile_of[n - 1])
                if n - 2 in tile_of:
                    j = tile_of[n - 2]
                    act.wait_ge(S("sw_o_done"), j + 1)
                    act.activation(o_hi[:, j], bank[6], ACT.Copy).then_inc(S("o_hi_ready"), 1)
                if n < 3 * SWKV:
                    done(C_S + 2 * n + 1)
                    b = bank[n % 2]
                    if n % 3 == 0:
                        g = n // 3
                        before(act, S("windows_turned"), g)
                        act.wait_ge(S("pads_zeroed"), 1)
                        act.activation(vT_pad[64:128, 64:64 + T], b[64:128, :], ACT.Copy).then_inc(S("vT_padded"), 1)
                    before(act, S("q_roped"), n - (n + 2) // 3)
                    before(act, S("k_roped"), (n + 2) // 3)
                    for r in range(0, 64 if n % 3 == 0 else P, 32):
                        last = act.activation(swapped[r ^ 32:(r ^ 32) + 32, :], b[r:r + 32, :], ACT.Copy)
                    last.then_inc(S("halves_swapped"), 1)
            gate_stage(C_GB, KT)

            def split_operand(n, src, gain=None):
                for kt in range(KT):
                    scale = 1.0 if gain is None else gains[:, gain + kt:gain + kt + 1]
                    act.activation(op_hi[:, kt, :], src[:, kt, :], ACT.Copy, scale=scale).then_inc(S("op_hi_ready"), 1)

            act.wait_ge(S("y_gated"), 2 * KT + 2)
            split_operand(2, res)
            with act.Fori(0, 8) as i:
                for x in range(2):
                    for j in range(2):
                        split_hi(C_O + 2 * x + j + LEAD, i, 4)
                    act.wait_ge(S("xT_turned"), i * 2 + (x + 1))
                    act.wait_ge(S("x1_ready"), i * 2 + (x + 1))
                    act.activation(xT_buf[:, x], bank[4 + x], ACT.Copy).then_inc(S("xT_copied"), 1)

            act.wait_ge(S("x1_ready"), KT + 2)
            split_operand(3, res, G_X)

            def rstd_rows(n, name):
                act.wait_ge(S("v_ready"), n + 1)
                act.activation(n_t[:, :], v_t[:, :], ACT.Ln).then_inc(S("ln_rows"), 1)
                act.wait_ge(S("ln_rows"), n + 1)
                act.activation(rstd_t[:, :], n_t[:, :], ACT.Exp, scale=-0.5).then_inc(S("rstd_rough"), 1)

            for u in range(XH):
                for j in range(2):
                    split_hi(C_XQ + 2 * u + j + LEAD)
                if u == 0:
                    rstd_rows(0, "x")
            split_hi(C_XO + 2)
            split_hi(C_XO + 3)
            for h in range(XH):
                act.wait_ge(S("x_max"), h + 1)
                if h:
                    act.wait_ge(S("x_turned"), h)
                for t in range(TT):
                    last = act.activation(p_x[:, t, :], psum[:, 2 + t // 2, (t % 2) * M:(t % 2 + 1) * M], ACT.Exp, scale=X_SCALE,
                                          bias=x_small[:, 0, t:t + 1], accum_out=x_small[:, 1, t:t + 1])
                last.then_inc(S("x_probs_done"), 1)
                if h:
                    act.wait_ge(S("x_o_done"), h)
                    act.activation(o_hi[:, h - 1, :], bank[7], ACT.Copy).then_inc(S("o_hi_ready"), 1)
                act.wait_ge(S("x_turned"), h + 1)
                act.activation(pT_x[:, :, :].rearrange("p m t -> p (m t)"), psum[:, 4:6].rearrange("p b n -> p (b n)"), ACT.Copy).then_inc(S("x_probs_T"), 1)
            act.wait_ge(S("x_o_done"), XH)
            act.activation(o_hi[:, XH - 1, :], bank[7], ACT.Copy).then_inc(S("o_hi_ready"), 1)
            for s in range(LEAD + 2, 8 + LEAD):
                split_hi(C_XO + s)

            act.wait_ge(S("x2_ready"), KT + 4)
            for kt in range(KT):
                act.activation(op_hi[:, kt, :], res[:, kt, :], ACT.Copy, scale=gains[:, G_FFN + kt:G_FFN + kt + 1]).then_inc(S("op_hi_ready"), 1)
                act.wait_ge(S("x2_turned"), kt + 1)
                act.activation(x2_nat[:, :, kt * P:(kt + 1) * P], bank[4 + kt % 2].rearrange("p (t d) -> p t d", t=TT), ACT.Copy).then_inc(S("x2_nat_ready"), 1)
            rstd_rows(1, "ffn")

            def ffn_block(v, k, last=False):
                def ahead(j):
                    if not (last and j + LEAD >= CF_BLOCK):
                        split_hi(C_F + j + LEAD, v, k)

                def a_high(f):
                    before(act, S("a_ready"), f + 1, v, FB)
                    act.activation(a_hi[:, f, :], a_t[:, :], ACT.Copy).then_inc(S("a_hi_ready"), 1)

                for f in range(FB):
                    ahead(4 * f)
                    ahead(4 * f + 1)
                    if f:
                        a_high(f - 1)
                    ahead(4 * f + 2)
                    ahead(4 * f + 3)
                    before(act, S("gate_scaled"), f + 1, v, FB)
                    act.activation(sg_t[:, :], g1_t[:, :], ACT.Sigmoid).then_inc(S("ffn_sig"), 1)
                ahead(16)
                ahead(17)
                a_high(FB - 1)
                for j in range(18, CF_BLOCK):
                    ahead(j)

            with act.Fori(0, NFB - 1) as b:
                ffn_block(b, CF_BLOCK)
            ffn_block(NFB - 1, CF_BLOCK, last=True)
            for t in range(TT):
                act.wait_ge(S("down_added"), 16 * NFB - 3 + t)
                if t:
                    act.wait_ge(S("final_squared"), t)
                act.activation(psum[:, 2:6].rearrange("p b n -> p (b n)"), x2_nat[:, t], ACT.Square, accum_out=f_stat[:, 0, t:t + 1]).then_inc(S("final_squared"), 1)
                act.wait_ge(S("final_v"), t + 1)
                act.activation(f_stat[:, 2, t:t + 1], f_stat[:, 1, t:t + 1], ACT.Ln).then_inc(S("final_ln"), 1)
                act.wait_ge(S("final_ln"), t + 1)
                act.activation(f_stat[:, 3, t:t + 1], f_stat[:, 2, t:t + 1], ACT.Exp, scale=-0.5).then_inc(S("final_rough"), 1)

        @block.vector
        def _(dve):
            def done(s, v=0, k=0):
                before(dve, chunk_done, s + 1, v, k)

            def subtract_hi(out, src, gain, hi, signal):
                dve.scalar_tensor_tensor(out, src, gain, hi.bitcast(F32), ALU.mult, ALU.subtract).then_inc(S(signal), 1)

            steps = [0]

            def link(ins):
                ins.then_inc(S("dve_step"), 1)
                steps[0] += 1
                dve.wait_ge(S("dve_step"), steps[0])

            def newton(v, r, t, signal):
                link(dve.tensor_tensor(t, r, r, ALU.mult))
                link(dve.scalar_tensor_tensor(t, t, -0.5, v, ALU.mult, ALU.mult))
                dve.scalar_tensor_tensor(r, t, 1.5, r, ALU.add, ALU.mult).then_inc(S(signal), 1)

            dve.sem_inc(S("y_gated"), 2)
            dve.sem_inc(S("x1_ready"), 2)
            dve.sem_inc(S("x2_ready"), 4)
            link(dve.memset(eps_col, EPS))

            def nat_scale(n):
                src = mem_nat[:, n] if n < MT else x_nat[:, n - MT]
                v, r = stat[:, 16 + n:17 + n], stat[:, 24 + n:25 + n]
                dve.wait_ge(S("squared"), n + 1)
                dve.tensor_scalar(v, stat[:, n:n + 1], 1.0 / D, EPS, ALU.mult, ALU.add).then_inc(S("mean_sq"), 1)
                dve.wait_ge(S("rstd_stat"), n + 1)
                newton(v, r, stat[:, 14:15], "nat_rstd")
                dve.wait_ge(S("nat_rstd"), n + 1)
                dve.tensor_scalar(src, src, r, None, ALU.mult).then_inc(S("nat_scaled"), 1)

            for n in range(MT):
                nat_scale(n)
            dve.wait_ge(S("gains_ready"), 1)
            l0, l1 = gains[:, G_LB:G_LB + 8], gains[:, G_LB + 8:G_LB + 16]
            lb, oml = lb_t[:, 0], lb_t[:, 1]
            link(dve.tensor_tensor(lb_t[:, 0], l0, l1, ALU.max))
            dve.tensor_tensor(lb_t[:, 1], l0, lb_t[:, 0], ALU.subtract)
            dve.tensor_tensor(lb_t[:, 2], l1, lb_t[:, 0], ALU.subtract).then_inc(S("lb_shifted"), 1)
            dve.wait_ge(S("lb_exp"), 1)
            link(dve.tensor_tensor(lb_t[:, 0], lb_t[:, 3], lb_t[:, 4], ALU.add))
            link(dve.reciprocal(lb_t[:, 0], lb_t[:, 0]))
            link(dve.tensor_tensor(lb, lb_t[:, 3], lb_t[:, 0], ALU.mult))
            link(dve.tensor_scalar(oml, lb, -1.0, 1.0, ALU.mult, ALU.add))

            def turn_lo(g):
                kt = g % KT
                if g < KT:
                    lo, hi, n, gain = mem_lo, mem_hi, M, G_MEM
                else:
                    lo, hi, n, gain = op_lo, op_hi, T, G_MIX
                dve.wait_ge(S("op_hi_ready"), g + 1)
                subtract_hi(lo[:, kt, :], bank[2 + kt % 2][:, 0:n], gains[:, gain + kt:gain + kt + 1], hi[:, kt, :], "op_ready")

            for g in range(KT):
                turn_lo(g)
            for t in range(TT):
                nat_scale(MT + t)
            for g in range(KT, 2 * KT):
                turn_lo(g)
            dve.wait_ge(S("kv_stored"), 64)
            dve.wait_ge(S("h_const_in"), 32)

            def head(h, par, project=True, mix=True, tail=True, s0=C_H, v=0, k=0):
                p, old = h - 1, 1 - par

                def d_level(l):
                    w = LEVELS[l - 1]
                    b, o = level_view(b_t[:, :], w), level_view(d_lev[:, l % 2], w)
                    n = T // (2 * w)
                    c = b[:, :, 0, w - 1:w].to_broadcast([P, n, w])
                    before(dve, S("qk_level"), max(l - 2, 0), p, NL)
                    dve.tensor_tensor(o[:, :, 0, :], c, b[:, :, 0, :], ALU.subtract)
                    dve.tensor_tensor(o[:, :, 1, :], b[:, :, 1, :], c, ALU.subtract).then_inc(S("d_level"), 1)

                def qk_level(l):
                    w = LEVELS[l - 1]
                    e, o = level_view(d_lev[:, l % 2], w), level_view(qk_lev[:, l % 2], w)
                    kk, qq = level_view(k_t[:, :], w), level_view(q_t[:, old], w)
                    dve.wait_ge(S("exp_level"), p * NL + l)
                    before(dve, S("level_done"), l - 1, p, NL + 1)
                    dve.tensor_tensor(o[:, :, 0, :], e[:, :, 0, :], kk[:, :, 0, :], ALU.mult)
                    dve.tensor_tensor(o[:, :, 1, :], e[:, :, 1, :], qq[:, :, 1, :], ALU.mult).then_inc(S("qk_level"), 1)

                def take_level(l):
                    dve.wait_ge(S("level_done"), p * (NL + 1) + (l + 1))
                    blocks = scores_a[:, :].rearrange("p (c t) -> p c t", c=NB)
                    got = bank[2 + l % 2].rearrange("p (c t) -> p c t", c=NB)
                    if l == 0:
                        before(dve, S("o_done"), 0, p, 1)
                        dve.tensor_tensor(blocks, got, ident[:, None, :].to_broadcast([P, NB, P]), ALU.mult).then_inc(S("level_taken"), 1)
                    else:
                        dve.wait_ge(S("level_taken"), p * (NL + 1) + l)
                        dve.sem_inc(S("level_due"), 1)
                        dve.copy_predicated(blocks, masks[:, l - 1:l, :].to_broadcast([P, NB, P]), got).then_inc(S("level_taken"), 1)

                if mix:
                    dve.wait_ge(S("f_sig"), p + 1)
                    before(dve, S("log_f"), 0, p, 1)
                    before(dve, S("k_ready"), 0, p, 1)
                    dve.tensor_scalar(f_t[:, :], sig_f[:, :], oml[:, bass.ds(p, 1)], lb[:, bass.ds(p, 1)], ALU.mult, ALU.add).then_inc(S("f_ready"), 1)
                    dve.wait_ge(S("f_ready"), p + 1)
                    before(dve, S("khat_ready"), 0, p, 1)
                    before(dve, S("level_done"), 0, p, NL + 1)
                    dve.tensor_scalar(k_t[:, :], f_t[:, :], -1.0, 1.0, ALU.mult, ALU.add).then_inc(S("k_ready"), 1)
                    dve.wait_ge(S("log_f"), p + 1)
                    before(dve, S("exp_b"), 0, p, 1)
                    before(dve, S("dk_ready"), 0, p, 1)
                    dve.tensor_tensor_scan(b_t[:, :], scan_mask[:, :], log_f[:, :], 0.0, ALU.mult, ALU.add).then_inc(S("b_ready"), 1)
                    dve.wait_ge(S("b_ready"), p + 1)
                    dve.wait_ge(S("k_ready"), p + 1)
                    d_level(1)
                    d_level(2)
                    qk_level(1)
                    d_level(3)
                    qk_level(2)
                    d_level(4)
                    take_level(0)
                if tail:
                    dve.wait_ge(S("o_rstd"), h - 1)
                    before(dve, S("o_gated"), 0, h - 2, 1)
                    dve.tensor_tensor(o1_t[:, :], bank[6], orstd_t[:, :], ALU.mult).then_inc(S("o_scaled"), 1)
                    dve.wait_ge(S("o_scaled"), h - 1)
                    before(dve, S("o_split"), 0, h - 2, 1)
                    dve.scalar_tensor_tensor(o2_t[:, :], o1_t[:, :], gains[:, bass.ds(h + (G_HN - 2), 1)], silu_g[:, par], ALU.mult, ALU.mult).then_inc(S("o_gated"), 1)
                if mix:
                    qk_level(3)
                    d_level(5)
                    take_level(1)
                    qk_level(4)
                    d_level(6)
                    take_level(2)
                    qk_level(5)
                    d_level(7)
                if tail:
                    dve.wait_ge(S("o_gated"), h - 1)
                    dve.wait_ge(S("o_hi_ready"), h - 1)
                    dve.tensor_tensor(o_lo[:, bass.ds(h - 2, 1), :], o2_t[:, None, :], o_hi[:, bass.ds(h - 2, 1), :].bitcast(F32), ALU.subtract).then_inc(S("o_split"), 1)
                if mix:
                    last = b_t[:, :].rearrange("p (c t) -> p c t", c=NB)
                    before(dve, S("kh_turned"), 0, p, 1)
                    dve.tensor_tensor(kh_t[:, :].rearrange("p (c t) -> p c t", c=NB), last[:, :, BLK - 1:BLK].to_broadcast([P, NB, BLK]), last, ALU.subtract).then_inc(S("dk_ready"), 1)
                    take_level(3)
                    qk_level(6)
                    qk_level(7)
                    take_level(4)
                    take_level(5)
                    dve.wait_ge(S("exp_khat"), p + 1)
                    dve.tensor_tensor(kh_t[:, :], kh_t[:, :], k_t[:, :], ALU.mult).then_inc(S("khat_ready"), 1)
                    dve.wait_ge(S("exp_b"), p + 1)
                    before(dve, S("o_done"), 0, p, 1)
                    dve.tensor_tensor(qe_t[:, :], q_t[:, old], exp_b[:, :], ALU.mult).then_inc(S("qe_ready"), 1)
                    take_level(6)
                    take_level(7)
                    dve.wait_ge(S("ds_done"), p + 1)
                    before(dve, S("o_done"), 0, p, 1)
                    dve.tensor_copy(state[:, 0, :], bank[7][:, 0:P]).then_inc(S("state_ready"), 1)
                    for c in range(1, NB - 1):
                        dve.wait_ge(S("state_ready"), p * (NB - 1) + c)
                        e = (c + 1) * BLK
                        dve.scalar_tensor_tensor(state[:, c, :], state[:, c - 1, :], exp_b[:, e - 1:e], bank[7][:, c * P:(c + 1) * P], ALU.mult, ALU.add).then_inc(S("state_ready"), 1)
                if project:
                    dve.wait_ge(S("v_turned"), h + 1)
                    dve.tensor_copy(v_nat[:, par], bank[4]).then_inc(S("v_nat_ready"), 1)
                    dve.wait_ge(S("g_sig"), h + 1)
                    if tail:
                        dve.wait_ge(S("o_gated"), h - 1)
                    dve.tensor_tensor(silu_g[:, par], sig_g[:, :], bank[1], ALU.mult).then_inc(S("silu_ready"), 1)

            head(0, 0, mix=False, tail=False)
            head(1, 1, tail=False, s0=C_H + 8)
            with dve.Fori(0, 3) as i:
                for x in range(2):
                    head(i * 2 + (2 + x), x, s0=C_H + 16 + 8 * x, v=i, k=16)
            head(8, 0, project=False)
            head(9, 1, project=False, mix=False)

            with dve.Fori(0, 4) as i:
                for x in range(4):
                    done(C_GA + 3 * x + 2, i, 12)
                    dve.wait_ge(S("gate_sig"), i * 4 + (x + 2))
                    dve.tensor_tensor(res[:, bass.ds(i * 4 + x, 1), :], gate_t[:, x % 2:x % 2 + 1, :], bank[1][:, None, :], ALU.mult).then_inc(S("y_gated"), 1)

            import_pi = 3.141592653589793
            magic = 12582912.0
            c1, c2 = 6.28125, 0.0019350051879882812
            c3 = 2 * import_pi - c1 - c2
            dve.memset(kT_pad[:, 0:64], 0.0)
            dve.memset(vT_pad[:, 0:64], 0.0).then_inc(S("pads_zeroed"), 1)
            dve.wait_ge(S("sw_in"), 48)
            link(dve.tensor_scalar(sw_cols[:, 1], sw_cols[:, 0], -1.0, None, ALU.mult))
            link(dve.tensor_copy(angle[:, :], pos_i[:, :]))
            link(dve.tensor_scalar(angle[:, :], angle[:, :], rope_cols[:, 0:1], None, ALU.mult))
            for n, (turn, add) in enumerate(((0.0, 0.0), (0.25, import_pi / 2))):
                if n:
                    dve.wait_ge(S("sine"), 1)
                link(dve.tensor_scalar(turns[:, :], angle[:, :], 0.5 / import_pi, turn, ALU.mult, ALU.add))
                link(dve.tensor_scalar(turns[:, :], turns[:, :], magic, None, ALU.add))
                link(dve.tensor_scalar(turns[:, :], turns[:, :], magic, None, ALU.subtract))
                link(dve.scalar_tensor_tensor(q_rot[:, :], turns[:, :], -c1, angle[:, :], ALU.mult, ALU.add))
                link(dve.scalar_tensor_tensor(q_rot[:, :], turns[:, :], -c2, q_rot[:, :], ALU.mult, ALU.add))
                link(dve.scalar_tensor_tensor(q_rot[:, :], turns[:, :], -c3, q_rot[:, :], ALU.mult, ALU.add))
                link(dve.tensor_scalar(q_rot[:, :], q_rot[:, :], add, 3.1415925, ALU.add, ALU.min))
                dve.tensor_scalar(turns[:, :], q_rot[:, :], -3.1415925, None, ALU.max).then_inc(S("angle_ready"), 1)
            dve.wait_ge(S("sine"), 2)
            link(dve.tensor_scalar(sin_t[:, :], sin_t[:, :], rope_cols[:, 1:2], None, ALU.mult))

            def sw_max(j):
                for x in range(2):
                    h = 2 * j + x
                    if x == 0:
                        dve.wait_ge(S("scores_done"), j + 1)
                    link(dve.memset(bank[2 + x][0:64, 0:64], NEVER))
                    link(dve.tensor_reduce(sw_small[:, x, 3, :], bank[2 + x].rearrange("p (t k) -> p t k", t=TT), AX.X, ALU.max))
                    dve.tensor_scalar(sw_small[:, x, 0, :], sw_small[:, x, 3, :], -SW_SCALE, sw_cols[:, 1, h:h + 1], ALU.mult, ALU.min).then_inc(S("sw_max"), 1)

            def sw_normalise(j):
                for x in range(2):
                    h = 2 * j + x
                    dve.wait_ge(S("probs_done"), h + 1)
                    link(dve.tensor_tensor(sw_small[:, x, 4, :], sw_small[:, x, 1, :], sw_small[:, x, 2, :], ALU.add))
                    link(dve.reciprocal(sw_small[:, x, 4, :], sw_small[:, x, 4, :]))
                    p = probs[:, x].rearrange("p (t k) -> p t k", t=TT)
                    dve.tensor_tensor(p, p, sw_small[:, x, 4, :, None].to_broadcast([P, TT, P]), ALU.mult).then_inc(S("probs_ready"), 1)

            tile_of = {3 * g + 1 + x: 2 * g + x for g in range(SWKV) for x in range(2)}
            for n in range(3 * SWKV + 2):
                if n - 2 in tile_of:
                    j = tile_of[n - 2]
                    dve.wait_ge(S("probs_turned"), j + 1)
                    before(dve, S("sw_o_done"), j)
                    dve.wait_ge(S("probs_T_ready"), 2 * j + 1)
                    dve.tensor_copy(probs_T[:, 1], bank[7]).then_inc(S("probs_T_ready"), 1)
                if n - 1 in tile_of:
                    sw_max(tile_of[n - 1])
                if n - 2 in tile_of:
                    j = tile_of[n - 2]
                    dve.wait_ge(S("o_hi_ready"), HEADS + j + 1)
                    dve.tensor_tensor(o_lo[:, j], bank[6], o_hi[:, j].bitcast(F32), ALU.subtract).then_inc(S("o_split"), 1)
                if n % 3 == 1 and n < 3 * SWKV:
                    dve.wait_ge(S("windows_turned"), n // 3 + 1)
                    before(dve, S("sw_o_done"), 2 * (n // 3))
                    dve.tensor_copy(v_win[:, :, :].rearrange("p n d -> p (n d)"), bank[4]).then_inc(S("v_win_ready"), 1)
                if n - 1 in tile_of:
                    sw_normalise(tile_of[n - 1])
                if n < 3 * SWKV:
                    r = slice(0, 64 if n % 3 == 0 else P)
                    done(C_S + 2 * n + 1)
                    dve.wait_ge(S("halves_swapped"), n + 1)
                    g, j = n // 3, 2 * (n // 3) + n % 3 - 1
                    if n % 3 == 0:
                        before(dve, S("scores_done"), 2 * g)
                        dst = kT_pad[0:64, 64:64 + T]
                    else:
                        before(dve, S("scores_done"), j)
                        dst = q_rot[:, :]
                    dve.tensor_tensor(dst, bank[n % 2][r, :], cos_t[r, :], ALU.mult).then_inc(S("rope_mul"), 1)
                    dve.wait_ge(S("rope_mul"), n + 1)
                    link(dve.tensor_tensor(swapped[r, :], swapped[r, :], sin_t[r, :], ALU.mult))
                    if n % 3 == 0:
                        link(dve.tensor_tensor(dst, dst, swapped[r, :], ALU.add))
                        dve.tensor_copy(kT_pad[64:128, 64:64 + T], dst).then_inc(S("k_roped"), 1)
                    else:
                        dve.tensor_tensor(dst, dst, swapped[r, :], ALU.add).then_inc(S("q_roped"), 1)

            with dve.Fori(0, 4) as i:
                for x in range(4):
                    m = i * 4 + x
                    done(C_GB + 3 * x + 2, i, 12)
                    dve.wait_ge(S("gate_sig"), i * 4 + (x + 2 + KT))
                    dve.tensor_tensor(gate_t[:, x % 2], gate_t[:, x % 2], bank[1], ALU.mult).then_inc(S("y_b_gated"), 1)
                    dve.wait_ge(S("y_b_gated"), i * 4 + (x + 1))
                    dve.tensor_tensor(res[:, bass.ds(m, 1), :], res[:, bass.ds(m, 1), :], gate_t[:, x % 2:x % 2 + 1, :], ALU.add).then_inc(S("y_gated"), 1)

            def split_operand(n, gain=None):
                for kt in range(KT):
                    dve.wait_ge(S("op_hi_ready"), n * KT + kt + 1)
                    g = 1.0 if gain is None else gains[:, gain + kt:gain + kt + 1]
                    subtract_hi(op_lo[:, kt, :], res[:, kt, :], g, op_hi[:, kt, :], "op_ready")

            dve.wait_ge(S("y_gated"), 2 * KT + 2)
            split_operand(2)
            link(dve.memset(sq_sum[:, :], 0.0))

            def add_square(src, m):
                dve.tensor_tensor(sq_t[:, None, :], src, src, ALU.mult).then_inc(S("sq_ready"), 1)
                dve.wait_ge(S("sq_ready"), m + 1)
                dve.tensor_tensor(sq_sum[:, :], sq_sum[:, :], sq_t[:, :], ALU.add).then_inc(S("sq_summed"), 1)

            with dve.Fori(0, 8) as i:
                for x in range(2):
                    m = i * 2 + x
                    tile = res[:, bass.ds(m, 1), :]
                    done(C_O + 2 * x + 1, i, 4)
                    dve.wait_ge(S("xT_copied"), i * 2 + (x + 3))
                    dve.tensor_tensor(tile, bank[x][:, None, :], xT_buf[:, x:x + 1, :], ALU.add).then_inc(S("x1_ready"), 1)
                    dve.wait_ge(S("x1_ready"), i * 2 + (x + 3))
                    add_square(tile, i * 2 + x)

            dve.wait_ge(S("x1_ready"), KT + 2)
            split_operand(3, G_X)

            def rstd_rows(n):
                dve.wait_ge(S("x_mean_done"), n + 1)
                dve.tensor_scalar(v_t[:, :], bank[6], 1.0 / D, EPS, ALU.mult, ALU.add).then_inc(S("v_ready"), 1)
                dve.wait_ge(S("rstd_rough"), n + 1)
                dve.wait_ge(S("v_ready"), n + 1)
                newton(v_t[:, :], rstd_t[:, :], n_t[:, :], "rstd_x")
                dve.wait_ge(S("rstd_x"), n + 1)

            rstd_rows(0)
            for u in range(XH):
                done(C_XQ + 2 * u + 1)
                dve.tensor_tensor(q_x[:, u, :], bank[u % 2], rstd_t[:, :], ALU.mult).then_inc(S("q_scaled"), 1)
            for h in range(XH):
                dve.wait_ge(S("x_scores_done"), h + 1)
                link(dve.tensor_reduce(x_small[:, 2, :], psum[:, 2:4].rearrange("p b (t k) -> p (b t) k", t=2), AX.X, ALU.max))
                dve.tensor_scalar(x_small[:, 0, :], x_small[:, 2, :], -X_SCALE, None, ALU.mult).then_inc(S("x_max"), 1)
                dve.wait_ge(S("x_probs_done"), h + 1)
                link(dve.reciprocal(x_small[:, 2, :], x_small[:, 1, :]))
                dve.tensor_tensor(p_x[:, :, :], p_x[:, :, :], x_small[:, 2, :, None].to_broadcast([P, TT, M]), ALU.mult).then_inc(S("x_probs_ready"), 1)
                if h:
                    dve.wait_ge(S("o_hi_ready"), 2 * HEADS + h)
                    dve.tensor_tensor(o_lo[:, h - 1, :], bank[7], o_hi[:, h - 1, :].bitcast(F32), ALU.subtract).then_inc(S("o_split"), 1)
            dve.wait_ge(S("o_hi_ready"), 2 * HEADS + XH)
            dve.tensor_tensor(o_lo[:, XH - 1, :], bank[7], o_hi[:, XH - 1, :].bitcast(F32), ALU.subtract).then_inc(S("o_split"), 1)
            link(dve.memset(sq_sum[:, :], 0.0))
            with dve.Fori(0, 2) as i:
                for x in range(RING):
                    done(C_XO + x, i, 4)
                    for j in range(2):
                        m = i * 8 + (2 * x + j)
                        tile = res[:, bass.ds(m, 1), :]
                        dve.tensor_tensor(tile, bank[x % 2 * 2 + j][:, None, :], tile, ALU.add).then_inc(S("x2_ready"), 1)
                        dve.wait_ge(S("x2_ready"), i * 8 + (2 * x + j + 5))
                        add_square(tile, i * 8 + (2 * x + j + KT))

            dve.wait_ge(S("x2_ready"), KT + 4)
            split_operand(4, G_FFN)
            rstd_rows(1)

            def ffn_block(v, k, last=False):
                for f in range(FB):
                    done(C_F + 4 * f + 1, v, k)
                    dve.tensor_tensor(g1_t[:, :], bank[0], rstd_t[:, :], ALU.mult).then_inc(S("gate_scaled"), 1)
                    done(C_F + 4 * f + 3, v, k)
                    dve.tensor_tensor(u1_t[:, :], bank[1], rstd_t[:, :], ALU.mult).then_inc(S("up_scaled"), 1)
                    before(dve, S("ffn_sig"), f + 1, v, FB)
                    dve.tensor_tensor(g1_t[:, :], g1_t[:, :], sg_t[:, :], ALU.mult).then_inc(S("ffn_silu"), 1)
                    before(dve, S("ffn_silu"), f + 1, v, FB)
                    before(dve, S("up_scaled"), f + 1, v, FB)
                    dve.tensor_tensor(a_t[:, :], g1_t[:, :], u1_t[:, :], ALU.mult).then_inc(S("a_ready"), 1)
                    before(dve, S("a_hi_ready"), f + 1, v, FB)
                    before(dve, S("a_ready"), f + 1, v, FB)
                    dve.tensor_tensor(a_lo[:, f, :], a_t[:, :], a_hi[:, f, :].bitcast(F32), ALU.subtract).then_inc(S("a_split"), 1)
                for d in range(4):
                    banks = (2, 3, 4, 5) if d % 2 == 0 else (0, 1, 6, 7)
                    done(C_F + 16 + 2 * d + 1, v, k)
                    for t in range(TT):
                        o = x2_nat[:, t, d * 512:(d + 1) * 512]
                        dve.tensor_tensor(o, o, bank[banks[t]], ALU.add).then_inc(S("down_added"), 1)

            dve.wait_ge(S("x2_nat_ready"), KT)
            with dve.Fori(0, NFB) as b:
                ffn_block(b, CF_BLOCK)
            dve.wait_ge(S("g_final_in"), 16)
            for t in range(TT):
                v, r = f_stat[:, 1, t:t + 1], f_stat[:, 3, t:t + 1]
                dve.wait_ge(S("final_squared"), t + 1)
                dve.tensor_scalar(v, f_stat[:, 0, t:t + 1], 1.0 / D, EPS, ALU.mult, ALU.add).then_inc(S("final_v"), 1)
                dve.wait_ge(S("final_rough"), t + 1)
                newton(v, r, f_stat[:, 4, t:t + 1], "final_rstd")
                dve.wait_ge(S("final_rstd"), t + 1)
                dve.scalar_tensor_tensor(x2_nat[:, t], x2_nat[:, t], r, g_final[:, :], ALU.mult, ALU.mult).then_inc(S("out_ready"), 1)


_INS = ["x", "mem", "positions", "norm_mix", "w_in", "hg_lower", "hg_norm", "sw_sinks", "w_proj_a", "w_proj_b",
        "w_out", "norm_x", "norm_mem", "wq_x", "wk_x", "wv_x", "wo_x", "norm_ffn", "w_gate", "w_up", "w_down",
        "norm_final"]


def constants():
    import numpy as np

    consts = np.zeros((P, P + T + 2), np.float32)
    consts[:, 0:P] = np.eye(P)
    consts[:, P:P + T] = np.arange(T) % BLK != 0
    half = HD // 2
    j = np.arange(P) % half
    consts[:, P + T] = np.float32(10000.0) ** (-j.astype(np.float32) / np.float32(half))
    consts[:, P + T + 1] = np.where(np.arange(P) % HD < half, -1.0, 1.0)
    masks = np.zeros((P, NL, P), np.int32)
    s, t = np.arange(P)[:, None], np.arange(P)[None, :]
    for n, w in enumerate(LEVELS):
        masks[:, n] = (s // (2 * w) == t // (2 * w)) & (s % (2 * w) < w) & (t % (2 * w) >= w)
    return {"consts": consts, "masks": masks}


def kernel(**inputs):
    import numpy as np
    import concourse.bacc as bacc
    from concourse.bass_utils import run_bass_kernel_spmd

    nc = bacc.Bacc("TRN2", target_bir_lowering=False, num_devices=1)
    arrays = {name: np.ascontiguousarray(inputs[name]) for name in _INS}
    arrays.update(constants())
    feed, args = {}, {}
    for name, array in arrays.items():
        feed["in_" + name] = array
        args[name] = nc.dram_tensor("in_" + name, array.shape, mybir.dt.from_np(array.dtype), kind="ExternalInput").ap()
    result = nc.dram_tensor("out", (1, T, D), F32, kind="ExternalOutput").ap()
    build_trunk(nc, args, result)
    return run_bass_kernel_spmd(nc, [feed], core_ids=[0]).results[0]["out"]
```

```python
from contextlib import ExitStack

import concourse.bass as bass
from concourse import mybir

P = 128
D = 2048
T = 512
M = 256
KT = D // P
TT = T // P
MT = M // P
EPS = 1e-6
HEADS = 8
BLK = 128
NB = T // BLK
LEVELS = [64, 32, 16, 8, 4, 2, 1]
NL = len(LEVELS)
SWH, SWKV, HD = 16, 4, 64
WIN = 128
XH = 4
DFF = 5632
FB = 4
NFB = DFF // (P * FB)
SW_SCALE = HD ** -0.5
X_SCALE = P ** -0.5
NEVER = -3.0e38

Q_A, F_A, I_A, G_A = 0, 1024, 2048, 3072
Q_B, K_B, V_B = 4096, 5120, 5376
GATE_A, GATE_B = 5632, 7680

CK = 8
RING = 4
LEAD = 2
C_K, C_V, C_H, C_GA, C_S, C_GB, C_O, C_XQ, C_XO, C_F = 0, 8, 16, 80, 128, 152, 200, 232, 240, 248
CF_BLOCK = 2 * 2 * FB + 8
C_END = C_F + NFB * CF_BLOCK
LAST_GROUPS = [(0, 0, 2), (0, 1, 3), (1, 0, 6), (1, 1, 7), (0, 2, 4), (0, 3, 5), (1, 2, 0), (1, 3, 1),
               (2, 0, 2), (2, 1, 3), (2, 2, 4), (2, 3, 5), (3, 0, 6), (3, 1, 7), (3, 2, 0), (3, 3, 1)]
GAINED = [n for n, (_, d, _) in enumerate(LAST_GROUPS) if d < 3]

G_MIX, G_X, G_FFN, G_MEM, G_LB, G_HN, G_ROWS = 0, 16, 32, 48, 64, 80, 88

ALU = mybir.AluOpType
ACT = mybir.ActivationFunctionType
AX = mybir.AxisListType
F32 = mybir.dt.float32
F32R = mybir.dt.float32r
I32 = mybir.dt.int32
KB = 1024



def level_view(t, w):
    return t.rearrange("p (b s w) -> p b s w", s=2, w=w)


def build_trunk(nc, a, out):
    ctx = ExitStack()
    with ctx:
        base = (nc.sbuf_base + 63) // 64 * 64

        def at(name, off, shape, dt):
            return nc.alloc_sbuf_tensor_at(name, shape, dt, offset=base + int(off))

        sems = {}

        def S(name):
            if name not in sems:
                sems[name] = ctx.enter_context(nc.semaphore(name))
            return sems[name]

        op_hi = at("op_hi", 0, [P, KT, T], F32R)
        op_lo = at("op_lo", 32 * KB, [P, KT, T], F32R)
        x_nat = at("x_nat", 64 * KB, [P, TT, D], F32)
        res = at("res", 64 * KB, [P, KT, T], F32)
        a_hi = at("a_hi", 64 * KB, [P, FB, T], F32R)
        a_lo = at("a_lo", 72 * KB, [P, FB, T], F32R)
        mem_hi = at("mem_hi", 96 * KB, [P, KT, M], F32R)
        mem_lo = at("mem_lo", 112 * KB, [P, KT, M], F32R)
        o_hi = at("o_hi", 96 * KB, [P, HEADS, T], F32R)
        o_lo = at("o_lo", 112 * KB, [P, HEADS, T], F32R)
        x2_nat = at("x2_nat", 96 * KB, [P, TT, D], F32)
        w_raw = at("w_raw", 128 * KB, [P, RING, CK * P], F32)
        w_hi = at("w_hi", 144 * KB, [P, RING, CK * P], F32R)
        w_lo = at("w_lo", 160 * KB, [P, RING, CK * P], F32R)
        ident = at("ident", 176 * KB, [P, P], F32)
        ones = at("ones", 176.5 * KB, [P, P], F32)
        gain_rows = at("gain_rows", 177 * KB, [P, P], F32)
        gains = at("gains", 177.5 * KB, [P, G_ROWS], F32)
        stat = at("stat", 177.5 * KB + 384, [P, 32], F32)
        SCR = 178 * KB
        mem_nat = at("mem_nat", SCR, [P, MT, D], F32)
        kv_mem = at("kv_mem", SCR + 16 * KB, [P, 4, 512], F32)
        mem_diag = at("mem_diag", SCR + 24 * KB, [P, MT, P], F32)
        mem_rstd = at("mem_rstd", SCR + 25 * KB, [P, M], F32)
        square_out = at("square_out", 0, [P, D], F32)
        lb_t = at("lb_t", SCR + 29.5 * KB, [P, 5, HEADS], F32)
        HB = 64 * KB
        q_t = at("q_t", HB, [P, 2, T], F32)
        v_nat = at("v_nat", HB + 4 * KB, [P, 2, T], F32)
        silu_g = at("silu_g", HB + 8 * KB, [P, 2, T], F32)
        sig_f = at("sig_f", HB + 12 * KB, [P, T], F32)
        f_t = at("f_t", HB + 14 * KB, [P, T], F32)
        log_f = at("log_f_t", HB + 16 * KB, [P, T], F32)
        k_t = at("k_t", HB + 18 * KB, [P, T], F32)
        b_t = at("b_t", HB + 20 * KB, [P, T], F32)
        exp_b = at("exp_b_t", HB + 22 * KB, [P, T], F32)
        d_lev = at("d_lev", HB + 24 * KB, [P, 2, T], F32)
        qk_lev = at("qk_lev", HB + 28 * KB, [P, 2, T], F32)
        h_scr = SCR
        scores_a = at("scores_a", h_scr, [P, T], F32)
        qe_t = at("qe_t", h_scr + 2 * KB, [P, T], F32)
        kh_t = at("kh_t", h_scr + 4 * KB, [P, T], F32)
        kh_nat = at("kh_nat", h_scr + 6 * KB, [P, T], F32)
        vT_t = at("vT_t", h_scr + 8 * KB, [P, T], F32)
        osq_t = at("osq_t", h_scr + 10 * KB, [P, T], F32)
        orstd_t = at("orstd_t", h_scr + 12 * KB, [P, T], F32)
        o1_t = at("o1_t", h_scr + 14 * KB, [P, T], F32)
        o2_t = at("o2_t", h_scr + 16 * KB, [P, T], F32)
        state = at("state_t", h_scr + 18 * KB, [P, NB - 1, P], F32)
        sig_g = at("sig_g", h_scr + 19.5 * KB, [P, T], F32)
        scan_mask = at("scan_mask", h_scr + 21.5 * KB, [P, T], F32)
        masks = at("masks", h_scr + 23.5 * KB, [P, NL, BLK // 2], I32)
        gate_t = at("gate_t", SCR + 25.5 * KB, [P, 2, T], F32)

        eps_col = stat[:, 31:32]
        cos_t = at("cos_t", SCR, [P, T], F32)
        sin_t = at("sin_t", SCR + 2 * KB, [P, T], F32)
        q_rot = at("q_rot", SCR + 4 * KB, [P, T], F32)
        swapped = at("swapped_t", SCR + 6 * KB, [P, T], F32)
        probs = at("probs_t", SCR + 8 * KB, [P, 2, 512], F32)
        probs_T = at("probs_T", SCR + 12 * KB, [P, 2, 512], F32)
        v_win = at("v_win", SCR + 16 * KB, [P, T // 64, HD], F32)
        kT_pad = at("kT_pad", SCR + 18 * KB, [P, 64 + T], F32)
        vT_pad = at("vT_pad", SCR + 18 * KB + 2304, [P, 64 + T], F32)
        sw_cols = at("sw_cols", SCR + 22.5 * KB, [P, 2, SWH], F32)
        sw_small = at("sw_small", SCR + 22.75 * KB, [P, 2, 5, TT], F32)
        rope_cols = at("rope_cols", SCR + 23 * KB, [P, 2], F32)
        angle = at("angle", SCR + 8 * KB, [P, T], F32)
        turns = at("turns", SCR + 10 * KB, [P, 2, T], F32)
        pos_i = at("pos_i", SCR + 12 * KB, [P, T], I32)
        x_cols = at("x_cols", SCR, [P, 2, TT, P], F32)
        xT_buf = at("xT_buf", SCR + 4 * KB, [P, 2, T], F32)
        sq_t = at("sq_t", SCR + 8 * KB, [P, 2, T], F32)
        sq_sum = at("sq_sum_t", SCR + 24 * KB, [P, T], F32)
        rstd_t = at("rstd_t", SCR + 26 * KB, [P, T], F32)
        v_t = at("v_t", SCR + 8 * KB, [P, T], F32)
        n_t = at("n_t", SCR + 10 * KB, [P, T], F32)
        kv_x = at("kv_x", SCR, [P, 4, 512], F32)
        q_x = at("q_x", SCR + 12 * KB, [P, XH, T], F32)
        p_x = at("p_x", SCR + 20 * KB, [P, TT, M], F32)
        pT_x = at("pT_x", SCR + 8 * KB, [P, MT, T], F32)
        x_small = at("x_small", SCR + 28 * KB, [P, 3, TT], F32)
        g1_t = at("g1_t", SCR, [P, T], F32)
        u1_t = at("u1_t", SCR + 2 * KB, [P, T], F32)
        sg_t = at("sg_t", SCR + 4 * KB, [P, T], F32)
        a_t = at("a_t", SCR + 6 * KB, [P, T], F32)
        w_hi_end = at("w_hi_end", 0, [P, 4, CK * P], F32R)
        w_lo_end = at("w_lo_end", 32 * KB, [P, 4, CK * P], F32R)
        g_final = at("g_final", SCR + 14 * KB, [P, D], F32)
        junk = at("junk", SCR + 12 * KB, [P, 512], F32)
        f_stat = at("f_stat", SCR + 28 * KB, [P, 5, TT], F32)
        f_squares = at("f_squares", SCR + 28.25 * KB, [P, TT, 4], F32)

        psum = ctx.enter_context(nc.psum_tensor("psum", [P, 8, 512], F32))
        bank = [psum[:, i] for i in range(8)]
        mean_bank = (bank[6], bank[2])

        w_loaded = [S(f"w_loaded{i}") for i in range(RING)]
        w_hi_ready, w_lo_ready = S("w_hi_ready"), S("w_lo_ready")
        chunk_done = S("chunk_done")

        mem_kv_dram = nc.dram_tensor("mem_kv_scratch", [P, 4, 512], F32, kind="Internal").ap()

        block = ctx.enter_context(nc.Block())

        def before(eng, semaphore, count, v=0, k=0):
            if isinstance(v, int):
                count, v = count + v * k, 0
                if count > 0:
                    eng.wait_ge(semaphore, count)
            else:
                eng.wait_ge(semaphore, v * k + count)

        def cols(w, c0, width, k0=0, nk=CK):
            v = w.rearrange("(k p) n -> p k n", p=P)[:, k0:k0 + nk]
            return v[:, :, bass.ds(c0, width)]

        w_in = a["w_in"].rearrange("l d n -> (l d) n")

        @block.sync
        def _(sp):
            def load(src, s, v=0, k=0, shape="p (k n) -> p k n", **size):
                before(sp, w_lo_ready, s - RING + 1, v, k)
                if not isinstance(v, int):
                    sp.sem_inc(S("slot_free"), 1)
                dst = w_raw[:, s % RING].rearrange(shape, **size)
                sp.dma_start(dst, src).then_inc(w_loaded[s % RING], 16)

            def unit(w, c0, s, v=0, k=0, chunks=2):
                for j in range(chunks):
                    load(cols(w, c0, P, j * CK), s + j, v, k, n=P)

            sp.dma_start(ident[:, :], a["consts"][:, 0:P]).then_inc(S("ident_in"), 16)
            for half in range(2):
                for t in range(MT):
                    f = slice(half * D // 2, (half + 1) * D // 2)
                    sp.dma_start(mem_nat[:, t, f], a["mem"][0, t * P:(t + 1) * P, f]).then_inc(S(f"mem_in{half}"), 16)
            wk = a["wk_x"].rearrange("l d n -> (l d) n")
            wv = a["wv_x"].rearrange("l d n -> (l d) n").rearrange("(k p) n -> p k n", p=P)
            for s in range(RING):
                load(cols(wk, s // 2 * P, P, s % 2 * CK), C_K + s, n=P)
            for t in range(TT):
                sp.dma_start(x_nat[:, t], a["x"][0, t * P:(t + 1) * P, :]).then_inc(S(f"x_in{t}"), 16)
            for s in range(RING, 8):
                load(cols(wk, s // 2 * P, P, s % 2 * CK), C_K + s, n=P)
            for s in range(8):
                load(wv[:, 2 * s:2 * s + 2], C_V + s, n=512)
            for s in range(RING):
                load(cols(w_in, (Q_A, I_A)[s // 2], P, s % 2 * CK), C_H + s, n=P)
            for j in range(4):
                sp.wait_ge(S("kv_copied"), 4 + 2)
                sp.dma_start(mem_kv_dram[:, j], kv_mem[:, j]).then_inc(S("kv_stored"), 16)
            sp.wait_ge(S("kv_stored"), 64)
            sp.dma_start(scan_mask[:, :], a["consts"][:, P:P + T]).then_inc(S("h_const_in"), 16)
            sp.dma_start(masks[:, :, :], a["masks"]).then_inc(S("h_const_in"), 16)

            def head_loads(h, s0, v, k):
                for j, c0 in enumerate((Q_A, I_A, F_A, G_A)):
                    if isinstance(h, int) and h == 0 and j < 2:
                        continue
                    unit(w_in, h * P + c0, s0 + 2 * j, v, k)

            for h in range(2):
                head_loads(h, C_H + 8 * h, 0, 0)
            with sp.Fori(0, 3) as i:
                for x in range(2):
                    head_loads(i * 2 + (2 + x), C_H + 16 + 8 * x, i, 16)

            def gate_loads(gate0, w_proj, s0):
                def project(m0, x, v, k):
                    unit(w_proj, m0, s0 + 4 + 3 * x, v, k, chunks=1)

                def turn(m0, x, v=0, k=0):
                    project(m0, x, v, k)
                    unit(w_in, m0 + (2 * P + gate0), s0 + 5 + 3 * x, v, k)

                unit(w_in, gate0, s0)
                unit(w_in, gate0 + P, s0 + 2)
                with sp.Fori(0, 3) as i:
                    for x in range(4):
                        turn(i * (4 * P) + x * P, x, i, 12)
                for m in range(12, 14):
                    turn(m * P, m)
                unit(w_proj, 14 * P, s0 + 46, chunks=1)
                unit(w_proj, 15 * P, s0 + 47, chunks=1)

            gate_loads(GATE_A, a["w_proj_a"].rearrange("l d n -> (l d) n"), C_GA)
            for g in range(SWKV):
                s = C_S + 6 * g
                for j in range(2):
                    before(sp, w_lo_ready, s + j - RING + 1)
                    dst = w_raw[:, (s + j) % RING].rearrange("p (k n) -> p k n", n=P)
                    sp.dma_start(dst[:, :, HD:P], cols(w_in, V_B + g * HD, HD, j * CK)).then_inc(S("v_cols_in"), 16)
                    sp.wait_ge(S("v_cols_in"), 16 * (2 * g + j + 1))
                    sp.dma_start(dst[:, :, 0:HD], cols(w_in, K_B + g * HD, HD, j * CK)).then_inc(w_loaded[(s + j) % RING], 16)
                for x in range(2):
                    unit(w_in, Q_B + (2 * g + x) * P, s + 2 + 2 * x)
            gate_loads(GATE_B, a["w_proj_b"].rearrange("l d n -> (l d) n"), C_GB)
            w_out = a["w_out"].rearrange("l d n -> (l d) n")
            x_blocks = a["x"].rearrange("b (t p) d -> p (b t) d", p=P)
            sp.wait_ge(S("o_split"), 2 * HEADS)
            with sp.Fori(0, 8) as i:
                for x in range(2):
                    sp.wait_ge(S("xT_copied"), i * 2 + (x + 1))
                    sp.sem_inc(S("slot_free"), 1)
                    sp.dma_start(x_cols[:, x], x_blocks[:, :, bass.ds(i * (2 * P) + x * P, P)]).then_inc(S(f"x_cols_in{x}"), 16)
                    unit(w_out, i * (2 * P) + x * P, C_O + 2 * x, i, 4)
            wq = a["wq_x"].rearrange("l d n -> (l d) n")
            for u in range(XH):
                if u == 2:
                    sp.wait_ge(S("x1_ready"), KT + 2)
                    sp.dma_start(kv_x[:, :, :], mem_kv_dram[:, :, :]).then_inc(S("kv_in"), 16)
                unit(wq, u * P, C_XQ + 2 * u)
            wo = a["wo_x"].rearrange("l (k p) n -> p (l k) n", p=P)
            for s in range(8):
                load(wo[:, :, s * M:(s + 1) * M], C_XO + s, n=M)
            w_gate = a["w_gate"].rearrange("l d n -> (l d) n")
            w_up = a["w_up"].rearrange("l d n -> (l d) n")
            w_down = a["w_down"].rearrange("l (k p) n -> p (l k) n", p=P)

            def block_loads(b, v, k):
                for f in range(FB):
                    c0 = b * (FB * P) + f * P
                    unit(w_gate, c0, C_F + 4 * f, v, k)
                    unit(w_up, c0, C_F + 4 * f + 2, v, k)
                for d in range(4):
                    for j in range(2):
                        load(w_down[:, bass.ds(b * FB + 2 * j, 2), d * 512:(d + 1) * 512],
                             C_F + 16 + 2 * d + j, v, k, n=512)

            sp.wait_ge(S("x_turned"), XH)
            sp.dma_start(g_final[:, :], a["norm_final"].partition_broadcast(P)).then_inc(S("g_final_in"), 16)
            with sp.Fori(0, NFB) as b:
                block_loads(b, b, CF_BLOCK)
            for t in range(TT):
                sp.wait_ge(S("act_out_ready"), t + 1)
                sp.wait_ge(S("dve_out_ready"), t + 1)
                sp.dma_start(out[0, t * P:(t + 1) * P, :], x2_nat[:, t]).then_inc(S("stored"), 16)
            sp.wait_ge(S("stored"), 16 * TT)

        @block.gpsimd
        def _(pool):
            pool.memset(ones[:, :], 1.0).then_inc(S("ones_set"), 1)

            def split_lo(s, v=0, k=0):
                slot = s % RING
                before(pool, w_hi_ready, s + 1, v, k)
                before(pool, chunk_done, s - RING + 1, v, k)
                pool.tensor_tensor(w_lo[:, slot], w_raw[:, slot], w_hi[:, slot].bitcast(F32),
                                   ALU.subtract).then_inc(w_lo_ready, 1)

            for s in range(RING):
                split_lo(s)
            with pool.Fori(1, C_END // RING - 1) as i:
                for s in range(RING):
                    split_lo(s, i, RING)
            for s in range(4):
                pool.wait_ge(w_hi_ready, C_END - 4 + s + 1)
                pool.tensor_tensor(w_lo_end[:, s], w_raw[:, s], w_hi_end[:, s].bitcast(F32), ALU.subtract).then_inc(w_lo_ready, 1)

        @block.tensor
        def _(pe):
            def products(b, n, whl, xhl, start, stop):
                (wh, wl), (xh, xl) = whl, xhl
                pe.matmul(b[:, 0:n], wl, xh, start=start, stop=False)
                pe.matmul(b[:, 0:n], wh, xl, start=False, stop=False)
                return pe.matmul(b[:, 0:n], wh, xh, start=False, stop=stop)

            def chunk(b, s, v, k, hi, lo, k0, nk, n=T, split_base=None, middle=None):
                before(pe, w_lo_ready, s + 1, v, k)
                slot = s % RING
                for j in range(CK):
                    kt = k0 + j
                    if split_base is not None:
                        pe.wait_ge(S("op_ready"), split_base + kt + 1)
                    w = [t[:, slot, j * P:(j + 1) * P] for t in (w_hi, w_lo)]
                    last = products(b, n, w, (hi[:, kt, :], lo[:, kt, :]), kt == 0, kt == nk - 1)
                    if middle and j == CK // 2 - 1:
                        middle()
                last.then_inc(chunk_done, 1)

            def turned_bank(g):
                return bank[2 + g % 6]

            pe.wait_ge(S("ident_in"), 16)
            for kt in range(KT):
                if kt * 2 % KT == 0:
                    pe.wait_ge(S(f"mem_in{kt * 2 // KT}"), 16 * MT)
                if kt >= 6:
                    pe.wait_ge(S("op_ready"), kt - 5)
                for t in range(MT):
                    last = pe.transpose(turned_bank(kt)[:, t * P:(t + 1) * P], mem_nat[:, t, kt * P:(kt + 1) * P], ident[:, :])
                last.then_inc(S("turned"), 1)
                if kt == 5:
                    pe.wait_ge(S("gains_in"), 6 * 16)
                    pe.transpose(bank[0][:, 0:G_ROWS], gain_rows[0:G_ROWS, :], ident[0:G_ROWS, 0:G_ROWS]).then_inc(S("gains_turned"), 1)
            pe.wait_ge(S("gains_ready"), 1)
            for u in range(XH):
                if u >= 2:
                    pe.wait_ge(S("kv_copied"), u - 1)
                for j in range(2):
                    chunk(bank[u % 2], C_K + 2 * u + j, 0, 0, mem_hi, mem_lo, j * CK, KT, n=M,
                          split_base=0 if u == 0 else None)
                if u == 1:
                    pe.wait_ge(S("ones_set"), 1)
                    pe.wait_ge(S("mem_diag_ready"), MT)
                    for t in range(MT):
                        last = pe.matmul(bank[7][:, t * P:(t + 1) * P], ones[:, :], mem_diag[:, t, :], start=True, stop=True)
                    last.then_inc(S("mem_rstd_done"), 1)
            pe.wait_ge(S("kv_copied"), 4)
            for q in range(8):
                before(pe, w_lo_ready, C_V + q + 1)
                slot = (C_V + q) % RING
                for j in range(2):
                    kt = 2 * q + j
                    for t in range(MT):
                        w = [x[:, slot, j * 512:(j + 1) * 512] for x in (w_hi, w_lo)]
                        m = [x[:, kt, t * P:(t + 1) * P] for x in (mem_hi, mem_lo)]
                        last = products(bank[t], 512, m, w, kt == 0, kt == KT - 1)
                last.then_inc(chunk_done, 1)
            for kt in range(KT):
                g = KT + kt
                for t in range(TT):
                    if kt == 0:
                        pe.wait_ge(S("x_scaled"), t + 1)
                    if t == 0:
                        pe.wait_ge(S("op_ready"), g - 5)
                    last = pe.transpose(turned_bank(g)[:, t * P:(t + 1) * P], x_nat[:, t, kt * P:(kt + 1) * P], ident[:, :])
                last.then_inc(S("turned"), 1)

            def gate_ahead(s0, j, middle=None):
                chunk(bank[j // 2 * 4], s0 + j, 0, 0, op_hi, op_lo, j % 2 * CK, KT, middle=middle)

            def head(h, par, project=True, mix=True, tail=True, first=False, s0=C_H, v=0, k=0, gates={}):
                p, old = h - 1, 1 - par

                def level(l):
                    b = bank[2 + l % 2]
                    if l == 0:
                        pe.wait_ge(S("q_copied"), p + 1)
                        pe.wait_ge(S("k_ready"), p + 1)
                    else:
                        pe.wait_ge(S("qk_level"), p * NL + l)
                    before(pe, S("level_taken"), l - 1, p, NL + 1)
                    for c in range(NB):
                        f = slice(c * BLK, (c + 1) * BLK)
                        if l == 0:
                            last = pe.matmul(b[:, f], k_t[:, f], q_t[:, old, f], start=True, stop=True)
                        else:
                            w = LEVELS[l - 1]
                            right = level_view(qk_lev[:, l % 2, f], w)[:, :, 1, :]
                            o = b[:, c * BLK // 2:(c + 1) * BLK // 2].rearrange("p (b w) -> p b w", w=w)
                            last = pe.matmul(o, qk_lev[:, l % 2, f], right, start=True, stop=True)
                    last.then_inc(S("level_done"), 1)

                for c in range(CK):
                    if c == 1 and tail:
                        pe.wait_ge(S("o_squared"), h - 1)
                        pe.wait_ge(S("kh_nat_ready"), h - 1)
                        pe.matmul(bank[5], ones[:, :], osq_t[:, :], start=True, stop=True).then_inc(S("mean_done"), 1)
                    if mix and 2 <= c < 6:
                        level(2 * (c - 2))
                        level(2 * (c - 2) + 1)
                    if mix and c == 5:
                        pe.wait_ge(S("khat_ready"), p + 1)
                        before(pe, S("ln_mean"), 0, p, 1)
                        for x in range(NB):
                            f = slice(x * BLK, (x + 1) * BLK)
                            last = pe.transpose(bank[5][:, f], kh_t[:, f], ident[:, :])
                        last.then_inc(S("kh_turned"), 1)
                    if mix and c == 6:
                        pe.wait_ge(S("kh_nat_ready"), p + 1)
                        pe.wait_ge(S("v_nat_ready"), p + 1)
                        before(pe, S("state_ready"), 0, p, NB - 1)
                        for x in range(NB - 1):
                            f = slice(x * BLK, (x + 1) * BLK)
                            last = pe.matmul(bank[7][:, f], kh_nat[:, f], v_nat[:, old, f], start=True, stop=True)
                        last.then_inc(S("ds_done"), 1)
                    if mix and c == 7:
                        pe.wait_ge(S("level_taken"), (p + 1) * (NL + 1))
                        pe.wait_ge(S("state_ready"), (p + 1) * (NB - 1))
                        pe.wait_ge(S("qe_ready"), p + 1)
                        before(pe, S("o_scaled"), 0, p, 1)
                        for x in range(NB):
                            f = slice(x * BLK, (x + 1) * BLK)
                            last = pe.matmul(bank[6][:, f], v_nat[:, old, f], scores_a[:, f], start=True, stop=x == 0)
                            if x:
                                last = pe.matmul(bank[6][:, f], state[:, x - 1, :], qe_t[:, f], start=False, stop=True)
                        last.then_inc(S("o_done"), 1)
                    if c in gates:
                        if c == 0:
                            pe.wait_ge(S("f_sig"), HEADS)
                        gate_ahead(C_GA, gates[c])
                    if project and c == 6:
                        pe.wait_ge(S("vT_copied"), h + 1)
                        before(pe, S("v_nat_ready"), 0, h, 1)
                        for x in range(NB):
                            f = slice(x * BLK, (x + 1) * BLK)
                            last = pe.transpose(bank[4][:, f], vT_t[:, f], ident[:, :])
                        last.then_inc(S("v_turned"), 1)
                    if project:
                        if c == 0:
                            before(pe, S("f_sig"), 0, h, 1)
                        if c == 2:
                            before(pe, S("silu_ready"), 0, h, 1)
                        if c == 4:
                            pe.wait_ge(S("q_copied"), h + 1)
                        if c == 6:
                            pe.wait_ge(S("vT_copied"), h + 1)
                        chunk(bank[c // 2 % 2], s0 + c, v, k, op_hi, op_lo, c % 2 * CK, KT,
                              split_base=KT if first and c < 2 else None)

            pe.wait_ge(S("kv_copied"), XH + MT)
            head(0, 0, mix=False, tail=False, first=True)
            head(1, 1, tail=False, s0=C_H + 8)
            with pe.Fori(0, 3) as i:
                for x in range(2):
                    head(i * 2 + (2 + x), x, s0=C_H + 16 + 8 * x, v=i, k=16)
            head(8, 0, project=False, gates={0: 0, 2: 1, 3: 2})
            head(9, 1, project=False, mix=False, gates={1: 3})
            pe.wait_ge(S("silu_ready"), HEADS)

            def gate_stage(s0, m0, o_count):
                pe.wait_ge(S("o_split"), o_count)

                def project(m, s, v=0, k=0):
                    before(pe, S("y_gated"), m0 + m + 2, v, k // 3)
                    chunk(bank[1], s, v, k, o_hi, o_lo, 0, CK)

                def turn(m, v=0, k=0):
                    project(m, s0 + 4 + 3 * m, v, k)
                    before(pe, S("gate_sig"), m0 + m + 3, v, k // 3)
                    for j in range(2):
                        chunk(bank[0], s0 + 5 + 3 * m + j, v, k, op_hi, op_lo, j * CK, KT)

                with pe.Fori(0, 3) as i:
                    for x in range(4):
                        turn(x, i, 12)
                for m in range(12, 14):
                    turn(m)
                project(14, s0 + 46)
                project(15, s0 + 47)

            gate_stage(C_GA, 0, HEADS)

            def sw_scores(j):
                pe.wait_ge(S("q_roped"), j + 1)
                pe.wait_ge(S("k_roped"), j // 2 + 1)
                before(pe, S("probs_done"), 2 * j)
                for x in range(2):
                    r = slice(64 * x, 64 * x + 64)
                    for n in range(T // 64):
                        o = bank[2 + x][64 * (n % 2):64 * (n % 2) + 64, n // 2 * WIN:(n // 2 + 1) * WIN]
                        last = pe.matmul(o, q_rot[r, 64 * n:64 * n + 64], kT_pad[r, 64 * n:64 * n + WIN], start=True, stop=True)
                last.then_inc(S("scores_done"), 1)

            def sw_turn(j):
                pe.wait_ge(S("probs_ready"), 2 * (j + 1))
                before(pe, S("probs_T_ready"), 2 * j)
                for x in range(2):
                    for t in range(TT):
                        f = slice(t * P, (t + 1) * P)
                        last = pe.transpose(bank[5 + 2 * x][:, f], probs[:, x, f], ident[:, :])
                last.then_inc(S("probs_turned"), 1)

            def sw_values(j):
                pe.wait_ge(S("probs_T_ready"), 2 * (j + 1))
                pe.wait_ge(S("v_win_ready"), j // 2 + 1)
                before(pe, S("o_split"), HEADS + j)
                for x in range(2):
                    for n in range(T // 64):
                        f = slice(64 * n, 64 * n + 64)
                        last = pe.matmul(bank[6][64 * x:64 * x + 64, f], v_win[:, n, :], probs_T[:, x, f], start=True, stop=True)
                last.then_inc(S("sw_o_done"), 1)

            def sw_windows(g):
                pe.wait_ge(S("vT_padded"), g + 1)
                before(pe, S("v_win_ready"), g)
                for n in range(T // 64):
                    last = pe.transpose(bank[4][:, HD * n:HD * (n + 1)], vT_pad[64:128, 64 * n:64 * n + WIN], ident[64:128, 64:128])
                last.then_inc(S("windows_turned"), 1)

            tile_of = {3 * g + 1 + x: 2 * g + x for g in range(SWKV) for x in range(2)}
            for n in range(3 * SWKV + 2):
                turn = (lambda j=tile_of[n - 2]: sw_turn(j)) if n - 2 in tile_of else None
                if n < 3 * SWKV:
                    if n < 2:
                        pe.wait_ge(S("y_gated"), KT + 2) if n else pe.wait_ge(S("gate_sig"), KT + 1)
                    else:
                        pe.wait_ge(S("rope_mul"), n - 1)
                    chunk(bank[n % 2], C_S + 2 * n, 0, 0, op_hi, op_lo, 0, KT, middle=turn)
                elif n == 3 * SWKV:
                    pe.wait_ge(S("rope_mul"), n - 1)
                    gate_ahead(C_GB, 0, middle=turn)
                else:
                    pe.wait_ge(S("v_win_ready"), SWKV)
                    gate_ahead(C_GB, 2, middle=turn)
                if n - 1 in tile_of:
                    sw_scores(tile_of[n - 1])
                if n - 2 in tile_of:
                    sw_values(tile_of[n - 2])
                if n % 3 == 1 and n < 3 * SWKV:
                    sw_windows(n // 3)
                if n < 3 * SWKV:
                    chunk(bank[n % 2], C_S + 2 * n + 1, 0, 0, op_hi, op_lo, CK, KT)
                else:
                    gate_ahead(C_GB, 2 * (n - 3 * SWKV) + 1)
            pe.wait_ge(S("rope_mul"), 3 * SWKV)
            gate_stage(C_GB, KT, 2 * HEADS)

            with pe.Fori(0, 8) as i:
                for x in range(2):
                    pe.wait_ge(S(f"x_cols_in{x}"), i * 16 + 16)
                    pe.wait_ge(S("x1_ready"), i * 2 + (x + 1))
                    for t in range(TT):
                        last = pe.transpose(bank[4 + x][:, t * P:(t + 1) * P], x_cols[:, x, t, :], ident[:, :])
                    last.then_inc(S("xT_turned"), 1)
                    for j in range(2):
                        chunk(bank[x], C_O + 2 * x + j, i, 4, op_hi, op_lo, j * CK, KT,
                              split_base=2 * KT if x == 0 else None)

            def mean_square(n, count):
                pe.wait_ge(S("sq_summed"), count)
                pe.matmul(mean_bank[n], ones[:, :], sq_sum[:, :], start=True, stop=True).then_inc(S("x_mean_done"), 1)

            def x_scores(h):
                if h == 0:
                    pe.wait_ge(S("kv_in"), 16)
                else:
                    pe.wait_ge(S("x_probs_done"), h)
                pe.wait_ge(S("q_scaled"), h + 1)
                for t in range(TT):
                    o = psum[:, 2 + t // 2, (t % 2) * M:(t % 2 + 1) * M]
                    last = pe.matmul(o, q_x[:, h, t * P:(t + 1) * P], kv_x[:, h // 2, (h % 2) * M:(h % 2 + 1) * M], start=True, stop=True)
                last.then_inc(S("x_scores_done"), 1)

            def x_turn(h):
                pe.wait_ge(S("x_probs_ready"), h + 1)
                if h:
                    pe.wait_ge(S("x_probs_T"), h)
                for m in range(MT):
                    for t in range(TT):
                        last = pe.transpose(bank[4 + m][:, t * P:(t + 1) * P], p_x[:, t, m * P:(m + 1) * P], ident[:, :])
                last.then_inc(S("x_turned"), 1)

            def x_values(h):
                pe.wait_ge(S("x_probs_T"), h + 1)
                if h:
                    pe.wait_ge(S("o_split"), 2 * HEADS + h)
                for m in range(MT):
                    last = pe.matmul(bank[7], kv_x[:, 2 + m, h * P:(h + 1) * P], pT_x[:, m, :], start=m == 0, stop=m == MT - 1)
                last.then_inc(S("x_o_done"), 1)

            for u in range(XH + 1):
                if u < 2:
                    pe.wait_ge(S("x1_ready"), KT + 1 + u)
                elif u < XH:
                    pe.wait_ge(S("q_scaled"), u - 1)
                for j in range(2):
                    if u < XH:
                        chunk(bank[u % 2], C_XQ + 2 * u + j, 0, 0, op_hi, op_lo, j * CK, KT,
                              split_base=3 * KT if u == 0 else None)
                    if j == 0 and u:
                        x_scores(u - 1)
                    if j == 0 and u >= 2:
                        x_values(u - 2)
                if u == 0:
                    mean_square(0, KT)
                else:
                    x_turn(u - 1)
            x_values(XH - 1)
            with pe.Fori(0, 2) as i:
                for x in range(RING):
                    before(pe, w_lo_ready, C_XO + x + 1, i, 4)
                    pe.wait_ge(S("x2_ready"), i * 8 + (2 * x + 2))
                    for j in range(2):
                        b = bank[x % 2 * 2 + j]
                        for kt in range(XH):
                            pe.wait_ge(S("o_split"), 2 * HEADS + kt + 1)
                            f = slice(kt * M + j * P, kt * M + (j + 1) * P)
                            last = products(b, T, (w_hi[:, x, f], w_lo[:, x, f]), (o_hi[:, kt, :], o_lo[:, kt, :]), kt == 0, kt == XH - 1)
                    last.then_inc(chunk_done, 1)

            for kt in range(KT):
                pe.wait_ge(S("x2_ready"), kt + 5)
                if kt >= 4:
                    pe.wait_ge(S(f"x2_nat_ready{kt % 2}"), kt // 2 - 1)
                for t in range(TT):
                    last = pe.transpose(bank[4 + kt % 4][:, t * P:(t + 1) * P], res[:, kt, t * P:(t + 1) * P], ident[:, :])
                last.then_inc(S("x2_turned"), 1)
            mean_square(1, 2 * KT)

            def ffn_up(v, k):
                for f in range(FB):
                    for u, name in enumerate(("gate_scaled", "up_scaled")):
                        if f:
                            before(pe, S(name), f, v, FB)
                        else:
                            before(pe, S("down_added"), u + 1, v, 16)
                        for j in range(2):
                            chunk(bank[u], C_F + 4 * f + 2 * u + j, v, k, op_hi, op_lo, j * CK, KT,
                                  split_base=4 * KT if f == u == 0 else None)

            def ffn_down(v, k):
                for d in range(4):
                    banks = (2, 3, 4, 5) if d % 2 == 0 else (0, 1, 6, 7)
                    if d == 0:
                        for x in range(2):
                            pe.wait_ge(S(f"x2_nat_ready{x}"), KT // 2)
                    if d == 1:
                        before(pe, S("up_scaled"), FB, v, FB)
                    if d >= 2:
                        before(pe, S("down_added"), 4 * d, v, 16)
                    for j in range(2):
                        before(pe, w_lo_ready, C_F + 16 + 2 * d + j + 1, v, k)
                        if d == 0:
                            before(pe, S("a_split"), 2 * (j + 1), v, FB)
                        slot = (2 * d + j) % RING
                        for t in range(TT):
                            for x in range(2):
                                kt = 2 * j + x
                                w = [y[:, slot, x * 512:(x + 1) * 512] for y in (w_hi, w_lo)]
                                m = [y[:, kt, t * P:(t + 1) * P] for y in (a_hi, a_lo)]
                                last = products(bank[banks[t]], 512, m, w, kt == 0, kt == FB - 1)
                            if j and t < TT - 1:
                                last.then_inc(S("down_tile_done"), 1)
                        last.then_inc(chunk_done, 1)

            with pe.Fori(0, NFB - 1) as b:
                ffn_up(b, CF_BLOCK)
                ffn_down(b, CF_BLOCK)
            ffn_up(NFB - 1, CF_BLOCK)
            added = 16 * (NFB - 1) + 4
            pe.wait_ge(S("down_added"), added)
            for n, (t, d, b) in enumerate(LAST_GROUPS):
                if n == 6:
                    pe.wait_ge(S("up_scaled"), FB * NFB)
                if n >= 8:
                    other = [g[2] for g in LAST_GROUPS].index(b)
                    pe.wait_ge(S("down_added"), added + other + 1)
                for kt in range(FB):
                    c = 2 * d + kt // 2
                    pe.wait_ge(w_lo_ready, C_END - 8 + c + 1)
                    if n == 0:
                        pe.wait_ge(S("a_split"), FB * (NFB - 1) + kt + 1)
                    f = slice(kt % 2 * 512, (kt % 2 + 1) * 512)
                    w = (w_hi[:, c, f], w_lo[:, c, f]) if c < 4 else (w_hi_end[:, c - 4, f], w_lo_end[:, c - 4, f])
                    m = [y[:, kt, t * P:(t + 1) * P] for y in (a_hi, a_lo)]
                    last = products(bank[b], 512, m, w, kt == 0, kt == FB - 1)
                last.then_inc(S("last_group_done"), 1)

        @block.scalar
        def _(act):
            def split_hi(s, v=0, k=0):
                slot = s % RING
                before(act, w_loaded[slot], 16 * (s // RING + 1), v, 16 * k // RING)
                before(act, chunk_done, s - RING + 1, v, k)
                act.activation(w_hi[:, slot], w_raw[:, slot], ACT.Copy).then_inc(w_hi_ready, 1)

            def done(s, v=0, k=0):
                before(act, chunk_done, s + 1, v, k)

            act.sem_inc(S("gate_sig"), 1)
            act.sem_inc(S("xT_copied"), 2)

            for n, name in enumerate(("norm_mix", "norm_x", "norm_ffn", "norm_mem", "hg_lower")):
                rows = a[name].rearrange("l (k p) -> (l k) p", p=P)
                act.dma_start(gain_rows[n * KT:(n + 1) * KT, :], rows).then_inc(S("gains_in"), 16)
            act.dma_start(gain_rows[G_HN:G_ROWS, :], a["hg_norm"].rearrange("l (k p) -> (l k) p", p=P)).then_inc(S("gains_in"), 16)

            def square(n):
                src = mem_nat[:, n] if n < MT else x_nat[:, n - MT]
                if n == 0:
                    act.wait_ge(S("mem_in0"), 16 * MT)
                    act.wait_ge(S("mem_in1"), 16 * MT)
                if n >= MT:
                    act.wait_ge(S(f"x_in{n - MT}"), 16)
                if n >= 1:
                    act.wait_ge(S("squared"), n)
                act.activation(square_out[:, :], src, ACT.Square, accum_out=stat[:, n:n + 1]).then_inc(S("squared"), 1)

            def rough_rstd(n0, n1, count):
                act.wait_ge(S("mean_sq"), count)
                act.activation(stat[:, 8 + n0:8 + n1], stat[:, 16 + n0:16 + n1], ACT.Ln).then_inc(S("ln_stat"), 1)
                act.wait_ge(S("ln_stat"), count)
                act.activation(stat[:, 24 + n0:24 + n1], stat[:, 8 + n0:8 + n1], ACT.Exp, scale=-0.5).then_inc(S("rstd_stat"), 1)

            def turn_hi(g):
                kt = g % KT
                act.wait_ge(S("turned"), g + 1)
                if g < KT:
                    dst, n, gain = mem_hi, M, G_MEM
                else:
                    dst, n, gain = op_hi, T, G_MIX
                act.activation(dst[:, kt, :], bank[2 + g % 6][:, 0:n], ACT.Copy, scale=gains[:, gain + kt:gain + kt + 1]).then_inc(S("op_hi_ready"), 1)

            act.wait_ge(S("gains_turned"), 1)
            act.activation(gains[:, :], bank[0][:, 0:G_ROWS], ACT.Copy).then_inc(S("gains_ready"), 1)
            act.wait_ge(S("gains_ready"), 1)
            for g in range(KT):
                turn_hi(g)
                if g in (3, 6, 9, 12):
                    split_hi(C_K + g // 3 - 1)
            for t in range(MT):
                square(t)
            rough_rstd(0, MT, 1)
            act.wait_ge(S("lb_shifted"), 1)
            act.activation(lb_t[:, 3:5], lb_t[:, 1:3], ACT.Exp).then_inc(S("lb_exp"), 1)
            for s in range(RING - LEAD, 8):
                split_hi(C_K + LEAD + s)
                if s >= 4:
                    square(MT + s - 4)
            for q in range(8):
                split_hi(C_V + q + LEAD)
                if q == 0:
                    rough_rstd(MT, MT + TT, 2)
            done(C_V + 7)
            for t in range(MT):
                act.activation(kv_mem[:, 2 + t], bank[t], ACT.Copy, scale=stat[:, 24 + t:25 + t]).then_inc(S("kv_copied"), 1)
            act.wait_ge(S("squared"), MT + TT)
            for g in range(KT, 2 * KT):
                turn_hi(g)
            act.wait_ge(S("kv_stored"), 64)
            act.wait_ge(S("h_const_in"), 32)

            def head(h, par, project=True, mix=True, tail=True, s0=C_H, v=0, k=0, gates={}):
                p, old = h - 1, 1 - par

                def exp_level(l):
                    act.wait_ge(S("d_level"), p * NL + l)
                    act.activation(d_lev[:, l % 2], d_lev[:, l % 2], ACT.Exp).then_inc(S("exp_level"), 1)

                for c in range(CK):
                    if project:
                        split_hi(s0 + c + LEAD, v, k)
                    if c == 0 and mix:
                        act.wait_ge(S("f_ready"), p + 1)
                        act.activation(log_f[:, :], f_t[:, :], ACT.Ln).then_inc(S("log_f"), 1)
                    if c == 0 and tail:
                        act.wait_ge(S("o_done"), h - 1)
                        act.activation(osq_t[:, :], bank[6], ACT.Square).then_inc(S("o_squared"), 1)
                    if c == 1 and mix:
                        act.wait_ge(S("b_ready"), p + 1)
                        before(act, S("o_done"), 0, p, 1)
                        act.activation(exp_b[:, :], b_t[:, :], ACT.Exp).then_inc(S("exp_b"), 1)
                        exp_level(1)
                        exp_level(2)
                    if c == 2 and project:
                        done(s0 + 1, v, k)
                        act.activation(q_t[:, par], bank[0], ACT.Copy).then_inc(S("q_copied"), 1)
                    if c == 2 and tail:
                        act.wait_ge(S("mean_done"), h - 1)
                        act.activation(orstd_t[:, :], bank[5], ACT.Ln, scale=1.0 / P, bias=eps_col[:, :]).then_inc(S("ln_mean"), 1)
                        act.wait_ge(S("ln_mean"), h - 1)
                        act.activation(orstd_t[:, :], orstd_t[:, :], ACT.Exp, scale=-0.5).then_inc(S("o_rstd"), 1)
                    if c == 2 and mix:
                        exp_level(3)
                        exp_level(4)
                    if c == 3 and mix:
                        exp_level(5)
                        exp_level(6)
                        exp_level(7)
                    if c == 3 and tail:
                        act.wait_ge(S("o_gated"), h - 1)
                        act.activation(o_hi[:, bass.ds(h - 2, 1), :], o2_t[:, None, :], ACT.Copy).then_inc(S("o_hi_ready"), 1)
                    if c == 4 and project:
                        done(s0 + 3, v, k)
                        before(act, S("v_turned"), 0, h, 1)
                        act.activation(vT_t[:, :], bank[1], ACT.Copy).then_inc(S("vT_copied"), 1)
                    if c == 4 and mix:
                        act.wait_ge(S("dk_ready"), p + 1)
                        act.activation(kh_t[:, :], kh_t[:, :], ACT.Exp).then_inc(S("exp_khat"), 1)
                    if c == 5 and mix:
                        act.wait_ge(S("kh_turned"), p + 1)
                        before(act, S("ds_done"), 0, p, 1)
                        act.activation(kh_nat[:, :], bank[5], ACT.Copy).then_inc(S("kh_nat_ready"), 1)
                    if c == 6 and project:
                        done(s0 + 5, v, k)
                        before(act, S("f_ready"), 0, h, 1)
                        act.activation(sig_f[:, :], bank[0], ACT.Sigmoid).then_inc(S("f_sig"), 1)
                    if c in gates:
                        split_hi(C_GA + gates[c] + LEAD)
                if project:
                    done(s0 + 7, v, k)
                    before(act, S("silu_ready"), 0, h, 1)
                    act.activation(sig_g[:, :], bank[1], ACT.Sigmoid).then_inc(S("g_sig"), 1)

            def gate_sigmoid(s0, m):
                done(s0 + 2 * m + 1)
                if s0 == C_GB:
                    act.wait_ge(S("y_gated"), KT + 2)
                act.activation(gate_t[:, m], bank[4 * m], ACT.Sigmoid).then_inc(S("gate_sig"), 1)

            head(0, 0, mix=False, tail=False)
            head(1, 1, tail=False, s0=C_H + 8)
            with act.Fori(0, 3) as i:
                for x in range(2):
                    head(i * 2 + (2 + x), x, s0=C_H + 16 + 8 * x, v=i, k=16)
            head(8, 0, project=False, gates={1: 0, 3: 1, 5: 2})
            head(9, 1, project=False, mix=False, gates={2: 3})
            gate_sigmoid(C_GA, 0)
            gate_sigmoid(C_GA, 1)

            def gate_stage(s0, m0, between=None):
                def turn(m, v=0, k=0):
                    for j in range(3):
                        split_hi(s0 + 4 + 3 * m + j + LEAD, v, k)
                    before(act, chunk_done, s0 + 3 * m + 7, v, k)
                    before(act, S("y_gated"), m0 + m + 3, v, k // 3)
                    act.activation(gate_t[:, m % 2], bank[0], ACT.Sigmoid).then_inc(S("gate_sig"), 1)

                with act.Fori(0, 3) as i:
                    for x in range(4):
                        turn(x, i, 12)
                for m in range(12, 14):
                    turn(m)
                split_hi(s0 + 46 + LEAD)
                if between:
                    between()
                split_hi(s0 + 47 + LEAD)

            act.wait_ge(S("o_split"), HEADS)
            act.dma_start(pos_i[:, :], a["positions"].partition_broadcast(P).rearrange("p b t -> p (b t)")).then_inc(S("sw_in"), 16)
            act.dma_start(sw_cols[:, 0, :], a["sw_sinks"].partition_broadcast(P).rearrange("p l h -> p (l h)")).then_inc(S("sw_in"), 16)
            act.dma_start(rope_cols[:, :], a["consts"][:, P + T:P + T + 2]).then_inc(S("sw_in"), 16)
            gate_stage(C_GA, 0)

            for n in range(2):
                act.wait_ge(S("angle_ready"), n + 1)
                act.activation((sin_t, cos_t)[n][:, :], turns[:, n, :], ACT.Sin).then_inc(S("sine"), 1)

            def sw_exps(j):
                for x in range(2):
                    h = 2 * j + x
                    act.wait_ge(S("sw_max"), h + 1)
                    before(act, S("probs_turned"), j)
                    for t in range(TT):
                        f = slice(t * P, (t + 1) * P)
                        act.activation(probs[:, x, f], bank[2 + x][:, f], ACT.Exp, scale=SW_SCALE,
                                       bias=sw_small[:, x, 0, t:t + 1], accum_out=sw_small[:, x, 1, t:t + 1])
                    act.activation(sw_small[:, x, 2, :], sw_small[:, x, 0, :], ACT.Exp, bias=sw_cols[:, 0, h:h + 1]).then_inc(S("probs_done"), 1)

            tile_of = {3 * g + 1 + x: 2 * g + x for g in range(SWKV) for x in range(2)}
            for n in range(3 * SWKV + 2):
                split_hi(C_S + 2 * n + LEAD)
                if n - 2 in tile_of:
                    j = tile_of[n - 2]
                    act.wait_ge(S("probs_turned"), j + 1)
                    before(act, S("sw_o_done"), j)
                    act.activation(probs_T[:, 0], bank[5], ACT.Copy).then_inc(S("probs_T_ready"), 1)
                split_hi(C_S + 2 * n + 1 + LEAD)
                if n - 1 in tile_of:
                    sw_exps(tile_of[n - 1])
                if n - 2 in tile_of:
                    j = tile_of[n - 2]
                    act.wait_ge(S("sw_o_done"), j + 1)
                    act.activation(o_hi[:, j], bank[6], ACT.Copy).then_inc(S("o_hi_ready"), 1)
                if n < 3 * SWKV:
                    done(C_S + 2 * n + 1)
                    b = bank[n % 2]
                    if n % 3 == 0:
                        g = n // 3
                        before(act, S("windows_turned"), g)
                        act.wait_ge(S("pads_zeroed"), 1)
                        act.activation(vT_pad[64:128, 64:64 + T], b[64:128, :], ACT.Copy).then_inc(S("vT_padded"), 1)
                    before(act, S("q_roped"), n - (n + 2) // 3)
                    before(act, S("k_roped"), (n + 2) // 3)
                    for r in range(0, 64 if n % 3 == 0 else P, 32):
                        last = act.activation(swapped[r ^ 32:(r ^ 32) + 32, :], b[r:r + 32, :], ACT.Copy)
                    last.then_inc(S("halves_swapped"), 1)
                else:
                    gate_sigmoid(C_GB, n - 3 * SWKV)
            def split_operand(n, gain, tiles, signal, count):
                for kt in tiles:
                    scale = 1.0 if gain is None else gains[:, gain + kt:gain + kt + 1]
                    act.wait_ge(S(signal), count + kt + 1)
                    act.activation(op_hi[:, kt, :], res[:, kt, :], ACT.Copy, scale=scale).then_inc(S("op_hi_ready"), 1)

            def first_tiles():
                done(C_GB + 45)
                split_operand(2, None, range(6), "y_gated", KT + 2)

            gate_stage(C_GB, KT, between=first_tiles)
            split_operand(2, None, range(6, KT), "y_gated", KT + 2)
            with act.Fori(0, 8) as i:
                for x in range(2):
                    for j in range(2):
                        split_hi(C_O + 2 * x + j + LEAD, i, 4)
                    act.wait_ge(S("xT_turned"), i * 2 + (x + 1))
                    act.wait_ge(S("x1_ready"), i * 2 + (x + 1))
                    act.activation(xT_buf[:, x], bank[4 + x], ACT.Copy).then_inc(S("xT_copied"), 1)

            for j in range(2):
                done(C_O + 30 + j)
                split_operand(3, G_X, range(j * CK, (j + 1) * CK), "x1_ready", 2)

            def rstd_rows(n):
                act.wait_ge(S("v_ready"), n + 1)
                act.activation(n_t[:, :], v_t[:, :], ACT.Ln).then_inc(S("ln_rows"), 1)
                act.wait_ge(S("ln_rows"), n + 1)
                act.activation(rstd_t[:, :], n_t[:, :], ACT.Exp, scale=-0.5).then_inc(S("rstd_rough"), 1)

            def x_exps(h):
                act.wait_ge(S("x_max"), h + 1)
                if h:
                    act.wait_ge(S("x_turned"), h)
                for t in range(TT):
                    last = act.activation(p_x[:, t, :], psum[:, 2 + t // 2, (t % 2) * M:(t % 2 + 1) * M], ACT.Exp, scale=X_SCALE,
                                          bias=x_small[:, 0, t:t + 1], accum_out=x_small[:, 1, t:t + 1])
                last.then_inc(S("x_probs_done"), 1)

            def x_out_hi(h):
                act.wait_ge(S("x_o_done"), h + 1)
                act.activation(o_hi[:, h, :], bank[7], ACT.Copy).then_inc(S("o_hi_ready"), 1)

            for u in range(XH + 1):
                split_hi(C_XQ + 2 * u + LEAD)
                if u:
                    x_exps(u - 1)
                if u >= 2:
                    x_out_hi(u - 2)
                split_hi(C_XQ + 2 * u + 1 + LEAD)
                if u == 0:
                    rstd_rows(0)
                else:
                    act.wait_ge(S("x_turned"), u)
                    act.activation(pT_x[:, :, :].rearrange("p m t -> p (m t)"), psum[:, 4:6].rearrange("p b n -> p (b n)"), ACT.Copy).then_inc(S("x_probs_T"), 1)
            x_out_hi(XH - 1)
            for s in range(8):
                if s + 4 < 8 + LEAD:
                    split_hi(C_XO + s + 4)
                split_operand(4, G_FFN, range(2 * s, 2 * s + 2), "x2_ready", 4)
                act.wait_ge(S("sq_summed"), KT + 2 * s)
                for m in range(2 * s, 2 * s + 2):
                    act.activation(sq_t[:, m % 2, :], res[:, m, :], ACT.Square).then_inc(S("sq_ready"), 1)

            done(C_XO + 7)
            for kt in range(0, KT, 2):
                act.wait_ge(S("x2_turned"), kt + 1)
                act.activation(x2_nat[:, :, kt * P:(kt + 1) * P], bank[4 + kt % 4].rearrange("p (t d) -> p t d", t=TT), ACT.Copy).then_inc(S("x2_nat_ready0"), 1)
            rstd_rows(1)

            def ffn_block(v, k, last=False):
                def ahead(j):
                    if not (last and j + LEAD >= CF_BLOCK):
                        split_hi(C_F + j + LEAD, v, k)

                def a_high(f):
                    before(act, S("a_ready"), f + 1, v, FB)
                    act.activation(a_hi[:, f, :], a_t[:, :], ACT.Copy).then_inc(S("a_hi_ready"), 1)

                for f in range(FB):
                    ahead(4 * f)
                    ahead(4 * f + 1)
                    if f:
                        a_high(f - 1)
                    ahead(4 * f + 2)
                    ahead(4 * f + 3)
                    before(act, S("gate_scaled"), f + 1, v, FB)
                    act.activation(sg_t[:, :], g1_t[:, :], ACT.Sigmoid).then_inc(S("ffn_sig"), 1)
                ahead(16)
                ahead(17)
                a_high(FB - 1)
                if not last:
                    for j in range(18, CF_BLOCK):
                        ahead(j)

            with act.Fori(0, NFB - 1) as b:
                ffn_block(b, CF_BLOCK)
            ffn_block(NFB - 1, CF_BLOCK, last=True)

            def split_end(s):
                act.wait_ge(w_loaded[s], 16 * (C_END // RING))
                if s == 0:
                    done(C_END - 9)
                act.activation(w_hi_end[:, s], w_raw[:, s], ACT.Copy).then_inc(w_hi_ready, 1)

            split_end(0)
            split_end(1)
            for n, (t, d, _) in enumerate(LAST_GROUPS):
                act.wait_ge(S("down_added"), 16 * (NFB - 1) + 4 + n + 1)
                if n:
                    act.wait_ge(S("final_squared"), n)
                act.activation(junk[:, :], x2_nat[:, t, d * 512:(d + 1) * 512], ACT.Square,
                               accum_out=f_squares[:, t, d:d + 1]).then_inc(S("final_squared"), 1)
                if n < 2:
                    split_end(2 + n)
                if d == 3:
                    v, ln, r = [f_stat[:, x, t:t + 1] for x in (1, 2, 3)]
                    act.wait_ge(S("final_v"), t + 1)
                    act.activation(ln, v, ACT.Ln).then_inc(S("final_ln"), 1)
                    act.wait_ge(S("final_ln"), t + 1)
                    act.activation(r, ln, ACT.Exp, scale=-0.5).then_inc(S("final_rough"), 1)
                    act.wait_ge(S("final_rstd"), t + 1)
                    act.wait_ge(S("gain_applied"), sum(g < n for g in GAINED))
                    o = x2_nat[:, t, 0:3 * 512]
                    act.activation(o, o, ACT.Copy, scale=r).then_inc(S("act_out_ready"), 1)

        @block.vector
        def _(dve):
            def done(s, v=0, k=0):
                before(dve, chunk_done, s + 1, v, k)

            def subtract_hi(out, src, gain, hi, signal):
                dve.scalar_tensor_tensor(out, src, gain, hi.bitcast(F32), ALU.mult, ALU.subtract).then_inc(S(signal), 1)

            steps = [0]

            def link(ins):
                ins.then_inc(S("dve_step"), 1)
                steps[0] += 1
                dve.wait_ge(S("dve_step"), steps[0])

            def newton(v, r, t, signal):
                link(dve.tensor_tensor(t, r, r, ALU.mult))
                link(dve.scalar_tensor_tensor(t, t, -0.5, v, ALU.mult, ALU.mult))
                dve.scalar_tensor_tensor(r, t, 1.5, r, ALU.add, ALU.mult).then_inc(S(signal), 1)

            dve.sem_inc(S("y_gated"), 2)
            dve.sem_inc(S("x1_ready"), 2)
            dve.sem_inc(S("x2_ready"), 4)
            dve.sem_inc(S("down_added"), 4)
            link(dve.memset(eps_col, EPS))

            def mean_squares(n0, n1):
                dve.wait_ge(S("squared"), n1)
                dve.tensor_scalar(stat[:, 16 + n0:16 + n1], stat[:, n0:n1], 1.0 / D, EPS, ALU.mult, ALU.add).then_inc(S("mean_sq"), 1)

            def refine(n0, n1, count):
                dve.wait_ge(S("rstd_stat"), count)
                newton(stat[:, 16 + n0:16 + n1], stat[:, 24 + n0:24 + n1], stat[:, 8 + n0:8 + n1], "nat_rstd")
                dve.wait_ge(S("nat_rstd"), count)

            dve.wait_ge(S("gains_ready"), 1)
            l0, l1 = gains[:, G_LB:G_LB + 8], gains[:, G_LB + 8:G_LB + 16]
            lb, oml = lb_t[:, 0], lb_t[:, 1]
            link(dve.tensor_tensor(lb_t[:, 0], l0, l1, ALU.max))
            dve.tensor_tensor(lb_t[:, 1], l0, lb_t[:, 0], ALU.subtract)
            dve.tensor_tensor(lb_t[:, 2], l1, lb_t[:, 0], ALU.subtract).then_inc(S("lb_shifted"), 1)
            def turn_lo(g):
                kt = g % KT
                if g < KT:
                    lo, hi, n, gain = mem_lo, mem_hi, M, G_MEM
                else:
                    lo, hi, n, gain = op_lo, op_hi, T, G_MIX
                dve.wait_ge(S("op_hi_ready"), g + 1)
                subtract_hi(lo[:, kt, :], bank[2 + g % 6][:, 0:n], gains[:, gain + kt:gain + kt + 1], hi[:, kt, :], "op_ready")

            for g in range(KT):
                turn_lo(g)
            mean_squares(0, MT)
            refine(0, MT, 1)
            for t in range(MT):
                dve.tensor_scalar(mem_diag[:, t, :], ident[:, :], stat[:, 24 + t:25 + t], None, ALU.mult).then_inc(S("mem_diag_ready"), 1)
            dve.wait_ge(S("lb_exp"), 1)
            link(dve.tensor_tensor(lb_t[:, 0], lb_t[:, 3], lb_t[:, 4], ALU.add))
            link(dve.reciprocal(lb_t[:, 0], lb_t[:, 0]))
            link(dve.tensor_tensor(lb, lb_t[:, 3], lb_t[:, 0], ALU.mult))
            link(dve.tensor_scalar(oml, lb, -1.0, 1.0, ALU.mult, ALU.add))
            dve.wait_ge(S("mem_rstd_done"), 1)
            link(dve.tensor_copy(mem_rstd[:, :], bank[7][:, 0:M]))
            for u in range(XH):
                done(C_K + 2 * u + 1)
                dve.tensor_tensor(kv_mem[:, u // 2, (u % 2) * M:(u % 2 + 1) * M], bank[u % 2][:, 0:M], mem_rstd[:, :], ALU.mult).then_inc(S("kv_copied"), 1)
            mean_squares(MT, MT + TT)
            refine(MT, MT + TT, 2)
            for t in range(TT):
                n = MT + t
                dve.tensor_scalar(x_nat[:, t], x_nat[:, t], stat[:, 24 + n:25 + n], None, ALU.mult).then_inc(S("x_scaled"), 1)
            for g in range(KT, 2 * KT):
                turn_lo(g)
            dve.wait_ge(S("kv_stored"), 64)
            dve.wait_ge(S("h_const_in"), 32)

            def head(h, par, project=True, mix=True, tail=True, s0=C_H, v=0, k=0):
                p, old = h - 1, 1 - par

                def d_level(l):
                    w = LEVELS[l - 1]
                    b, o = level_view(b_t[:, :], w), level_view(d_lev[:, l % 2], w)
                    n = T // (2 * w)
                    c = b[:, :, 0, w - 1:w].to_broadcast([P, n, w])
                    before(dve, S("qk_level"), max(l - 2, 0), p, NL)
                    dve.tensor_tensor(o[:, :, 0, :], c, b[:, :, 0, :], ALU.subtract)
                    dve.tensor_tensor(o[:, :, 1, :], b[:, :, 1, :], c, ALU.subtract).then_inc(S("d_level"), 1)

                def qk_level(l):
                    w = LEVELS[l - 1]
                    e, o = level_view(d_lev[:, l % 2], w), level_view(qk_lev[:, l % 2], w)
                    kk, qq = level_view(k_t[:, :], w), level_view(q_t[:, old], w)
                    dve.wait_ge(S("exp_level"), p * NL + l)
                    before(dve, S("level_done"), l - 1, p, NL + 1)
                    dve.tensor_tensor(o[:, :, 0, :], e[:, :, 0, :], kk[:, :, 0, :], ALU.mult)
                    dve.tensor_tensor(o[:, :, 1, :], e[:, :, 1, :], qq[:, :, 1, :], ALU.mult).then_inc(S("qk_level"), 1)

                def take_level(l):
                    dve.wait_ge(S("level_done"), p * (NL + 1) + (l + 1))
                    if l == 0:
                        blocks = scores_a[:, :].rearrange("p (c t) -> p c t", c=NB)
                        got = bank[2].rearrange("p (c t) -> p c t", c=NB)
                        before(dve, S("o_done"), 0, p, 1)
                        dve.tensor_tensor(blocks, got, ident[:, None, :].to_broadcast([P, NB, P]), ALU.mult).then_inc(S("level_taken"), 1)
                    else:
                        dve.wait_ge(S("level_taken"), p * (NL + 1) + l)
                        dve.sem_inc(S("level_due"), 1)
                        w = LEVELS[l - 1]
                        right = scores_a[:, :].rearrange("p (c b s w) -> p c b s w", c=NB, s=2, w=w)[:, :, :, 1, :]
                        got = bank[2 + l % 2][:, 0:T // 2].rearrange("p (c b w) -> p c b w", c=NB, w=w)
                        mask = masks[:, l - 1:l, :].rearrange("p l (b w) -> p l b w", w=w)
                        dve.copy_predicated(right, mask.to_broadcast([P, NB, BLK // (2 * w), w]), got).then_inc(S("level_taken"), 1)

                if mix:
                    dve.wait_ge(S("f_sig"), p + 1)
                    before(dve, S("log_f"), 0, p, 1)
                    before(dve, S("k_ready"), 0, p, 1)
                    dve.tensor_scalar(f_t[:, :], sig_f[:, :], oml[:, bass.ds(p, 1)], lb[:, bass.ds(p, 1)], ALU.mult, ALU.add).then_inc(S("f_ready"), 1)
                    dve.wait_ge(S("f_ready"), p + 1)
                    before(dve, S("khat_ready"), 0, p, 1)
                    before(dve, S("level_done"), 0, p, NL + 1)
                    dve.tensor_scalar(k_t[:, :], f_t[:, :], -1.0, 1.0, ALU.mult, ALU.add).then_inc(S("k_ready"), 1)
                    dve.wait_ge(S("log_f"), p + 1)
                    before(dve, S("exp_b"), 0, p, 1)
                    before(dve, S("dk_ready"), 0, p, 1)
                    dve.tensor_tensor_scan(b_t[:, :], scan_mask[:, :], log_f[:, :], 0.0, ALU.mult, ALU.add).then_inc(S("b_ready"), 1)
                    dve.wait_ge(S("b_ready"), p + 1)
                    dve.wait_ge(S("k_ready"), p + 1)
                    d_level(1)
                    d_level(2)
                    qk_level(1)
                    d_level(3)
                    qk_level(2)
                    d_level(4)
                    take_level(0)
                if tail:
                    dve.wait_ge(S("o_rstd"), h - 1)
                    dve.tensor_tensor(o1_t[:, :], bank[6], orstd_t[:, :], ALU.mult).then_inc(S("o_scaled"), 1)
                    dve.wait_ge(S("o_scaled"), h - 1)
                    dve.scalar_tensor_tensor(o2_t[:, :], o1_t[:, :], gains[:, bass.ds(h + (G_HN - 2), 1)], silu_g[:, par], ALU.mult, ALU.mult).then_inc(S("o_gated"), 1)
                if mix:
                    qk_level(3)
                    d_level(5)
                    take_level(1)
                    qk_level(4)
                    d_level(6)
                    take_level(2)
                    qk_level(5)
                    d_level(7)
                if tail:
                    dve.wait_ge(S("o_gated"), h - 1)
                    dve.wait_ge(S("o_hi_ready"), h - 1)
                    dve.tensor_tensor(o_lo[:, bass.ds(h - 2, 1), :], o2_t[:, None, :], o_hi[:, bass.ds(h - 2, 1), :].bitcast(F32), ALU.subtract).then_inc(S("o_split"), 1)
                if mix:
                    last = b_t[:, :].rearrange("p (c t) -> p c t", c=NB)
                    before(dve, S("kh_turned"), 0, p, 1)
                    dve.tensor_tensor(kh_t[:, :].rearrange("p (c t) -> p c t", c=NB), last[:, :, BLK - 1:BLK].to_broadcast([P, NB, BLK]), last, ALU.subtract).then_inc(S("dk_ready"), 1)
                    take_level(3)
                    qk_level(6)
                    qk_level(7)
                    take_level(4)
                    take_level(5)
                    dve.wait_ge(S("exp_khat"), p + 1)
                    dve.tensor_tensor(kh_t[:, :], kh_t[:, :], k_t[:, :], ALU.mult).then_inc(S("khat_ready"), 1)
                    dve.wait_ge(S("exp_b"), p + 1)
                    before(dve, S("o_done"), 0, p, 1)
                    dve.tensor_tensor(qe_t[:, :], q_t[:, old], exp_b[:, :], ALU.mult).then_inc(S("qe_ready"), 1)
                    take_level(6)
                    take_level(7)
                    dve.wait_ge(S("ds_done"), p + 1)
                    before(dve, S("o_done"), 0, p, 1)
                    dve.tensor_copy(state[:, 0, :], bank[7][:, 0:P]).then_inc(S("state_ready"), 1)
                    for c in range(1, NB - 1):
                        dve.wait_ge(S("state_ready"), p * (NB - 1) + c)
                        e = (c + 1) * BLK
                        dve.scalar_tensor_tensor(state[:, c, :], state[:, c - 1, :], exp_b[:, e - 1:e], bank[7][:, c * P:(c + 1) * P], ALU.mult, ALU.add).then_inc(S("state_ready"), 1)
                if project:
                    dve.wait_ge(S("v_turned"), h + 1)
                    dve.tensor_copy(v_nat[:, par], bank[4]).then_inc(S("v_nat_ready"), 1)
                    dve.wait_ge(S("g_sig"), h + 1)
                    if tail:
                        dve.wait_ge(S("o_gated"), h - 1)
                    dve.tensor_tensor(silu_g[:, par], sig_g[:, :], bank[1], ALU.mult).then_inc(S("silu_ready"), 1)

            head(0, 0, mix=False, tail=False)
            head(1, 1, tail=False, s0=C_H + 8)
            with dve.Fori(0, 3) as i:
                for x in range(2):
                    head(i * 2 + (2 + x), x, s0=C_H + 16 + 8 * x, v=i, k=16)
            head(8, 0, project=False)
            head(9, 1, project=False, mix=False)

            pi = 3.141592653589793
            magic = 12582912.0
            c1, c2 = 6.28125, 0.0019350051879882812
            c3 = 2 * pi - c1 - c2
            dve.memset(kT_pad[:, 0:64], 0.0)
            dve.memset(vT_pad[:, 0:64], 0.0).then_inc(S("pads_zeroed"), 1)
            dve.wait_ge(S("sw_in"), 48)
            link(dve.tensor_scalar(sw_cols[:, 1], sw_cols[:, 0], -1.0, None, ALU.mult))
            link(dve.tensor_copy(angle[:, :], pos_i[:, :]))
            link(dve.tensor_scalar(angle[:, :], angle[:, :], rope_cols[:, 0:1], None, ALU.mult))
            for n, (turn, add) in enumerate(((0.0, 0.0), (0.25, pi / 2))):
                link(dve.tensor_scalar(turns[:, n], angle[:, :], 0.5 / pi, turn, ALU.mult, ALU.add))
                link(dve.tensor_scalar(turns[:, n], turns[:, n], magic, None, ALU.add))
                link(dve.tensor_scalar(turns[:, n], turns[:, n], magic, None, ALU.subtract))
                link(dve.scalar_tensor_tensor(q_rot[:, :], turns[:, n], -c1, angle[:, :], ALU.mult, ALU.add))
                link(dve.scalar_tensor_tensor(q_rot[:, :], turns[:, n], -c2, q_rot[:, :], ALU.mult, ALU.add))
                link(dve.scalar_tensor_tensor(q_rot[:, :], turns[:, n], -c3, q_rot[:, :], ALU.mult, ALU.add))
                link(dve.tensor_scalar(q_rot[:, :], q_rot[:, :], add, 3.1415925, ALU.add, ALU.min))
                dve.tensor_scalar(turns[:, n], q_rot[:, :], -3.1415925, None, ALU.max).then_inc(S("angle_ready"), 1)
            def gate_product(m, s, v=0, k=0):
                done(s, v, k)
                before(dve, S("gate_sig"), m + 2, v, k // 3)
                if isinstance(v, int):
                    tile = res[:, m:m + 1, :]
                else:
                    tile = res[:, bass.ds(v * 4 + m, 1), :]
                dve.tensor_tensor(tile, gate_t[:, m % 2:m % 2 + 1, :], bank[1][:, None, :], ALU.mult).then_inc(S("y_gated"), 1)

            with dve.Fori(0, 3) as i:
                for x in range(4):
                    gate_product(x, C_GA + 4 + 3 * x, i, 12)
            for m in range(12, KT):
                gate_product(m, C_GA + min(4 + 3 * m, 32 + m))

            dve.wait_ge(S("sine"), 2)
            link(dve.tensor_scalar(sin_t[:, :], sin_t[:, :], rope_cols[:, 1:2], None, ALU.mult))

            def sw_max(j):
                for x in range(2):
                    h = 2 * j + x
                    if x == 0:
                        dve.wait_ge(S("scores_done"), j + 1)
                    link(dve.memset(bank[2 + x][0:64, 0:64], NEVER))
                    link(dve.tensor_reduce(sw_small[:, x, 3, :], bank[2 + x].rearrange("p (t k) -> p t k", t=TT), AX.X, ALU.max))
                    dve.tensor_scalar(sw_small[:, x, 0, :], sw_small[:, x, 3, :], -SW_SCALE, sw_cols[:, 1, h:h + 1], ALU.mult, ALU.min).then_inc(S("sw_max"), 1)

            def sw_normalise(j):
                for x in range(2):
                    h = 2 * j + x
                    dve.wait_ge(S("probs_done"), h + 1)
                    link(dve.tensor_tensor(sw_small[:, x, 4, :], sw_small[:, x, 1, :], sw_small[:, x, 2, :], ALU.add))
                    link(dve.reciprocal(sw_small[:, x, 4, :], sw_small[:, x, 4, :]))
                    p = probs[:, x].rearrange("p (t k) -> p t k", t=TT)
                    dve.tensor_tensor(p, p, sw_small[:, x, 4, :, None].to_broadcast([P, TT, P]), ALU.mult).then_inc(S("probs_ready"), 1)

            tile_of = {3 * g + 1 + x: 2 * g + x for g in range(SWKV) for x in range(2)}
            for n in range(3 * SWKV + 2):
                if n - 2 in tile_of:
                    j = tile_of[n - 2]
                    dve.wait_ge(S("probs_turned"), j + 1)
                    before(dve, S("sw_o_done"), j)
                    dve.wait_ge(S("probs_T_ready"), 2 * j + 1)
                    dve.tensor_copy(probs_T[:, 1], bank[7]).then_inc(S("probs_T_ready"), 1)
                if n - 1 in tile_of:
                    sw_max(tile_of[n - 1])
                if n - 2 in tile_of:
                    j = tile_of[n - 2]
                    dve.wait_ge(S("o_hi_ready"), HEADS + j + 1)
                    dve.tensor_tensor(o_lo[:, j], bank[6], o_hi[:, j].bitcast(F32), ALU.subtract).then_inc(S("o_split"), 1)
                if n % 3 == 1 and n < 3 * SWKV:
                    dve.wait_ge(S("windows_turned"), n // 3 + 1)
                    before(dve, S("sw_o_done"), 2 * (n // 3))
                    dve.tensor_copy(v_win[:, :, :].rearrange("p n d -> p (n d)"), bank[4]).then_inc(S("v_win_ready"), 1)
                if n - 1 in tile_of:
                    sw_normalise(tile_of[n - 1])
                if n < 3 * SWKV:
                    r = slice(0, 64 if n % 3 == 0 else P)
                    done(C_S + 2 * n + 1)
                    dve.wait_ge(S("halves_swapped"), n + 1)
                    g, j = n // 3, 2 * (n // 3) + n % 3 - 1
                    if n % 3 == 0:
                        before(dve, S("scores_done"), 2 * g)
                        dst = kT_pad[0:64, 64:64 + T]
                    else:
                        before(dve, S("scores_done"), j)
                        dst = q_rot[:, :]
                    dve.tensor_tensor(dst, bank[n % 2][r, :], cos_t[r, :], ALU.mult).then_inc(S("rope_mul"), 1)
                    dve.wait_ge(S("rope_mul"), n + 1)
                    link(dve.tensor_tensor(swapped[r, :], swapped[r, :], sin_t[r, :], ALU.mult))
                    if n % 3 == 0:
                        link(dve.tensor_tensor(dst, dst, swapped[r, :], ALU.add))
                        dve.tensor_copy(kT_pad[64:128, 64:64 + T], dst).then_inc(S("k_roped"), 1)
                    else:
                        dve.tensor_tensor(dst, dst, swapped[r, :], ALU.add).then_inc(S("q_roped"), 1)

            def split_operand(n, gain, tiles):
                for kt in tiles:
                    dve.wait_ge(S("op_hi_ready"), n * KT + kt + 1)
                    g = 1.0 if gain is None else gains[:, gain + kt:gain + kt + 1]
                    subtract_hi(op_lo[:, kt, :], res[:, kt, :], g, op_hi[:, kt, :], "op_ready")

            def merge(m, s, v=0, k=0):
                done(s, v, k)
                before(dve, S("gate_sig"), m + 2 + KT, v, k // 3)
                if isinstance(v, int):
                    tile = res[:, m:m + 1, :]
                else:
                    tile = res[:, bass.ds(v * 4 + m, 1), :]
                dve.tensor_tensor(gate_t[:, m % 2], gate_t[:, m % 2], bank[1], ALU.mult).then_inc(S("y_b_gated"), 1)
                before(dve, S("y_b_gated"), m + 1, v, k // 3)
                dve.tensor_tensor(tile, tile, gate_t[:, m % 2:m % 2 + 1, :], ALU.add).then_inc(S("y_gated"), 1)

            with dve.Fori(0, 3) as i:
                for x in range(4):
                    merge(x, C_GB + 4 + 3 * x, i, 12)
            for m in range(12, KT):
                merge(m, C_GB + min(4 + 3 * m, 32 + m))
                if m >= 13:
                    lo = 6 * (m - 13)
                    split_operand(2, None, range(lo, min(lo + 6, KT)))

            link(dve.memset(sq_sum[:, :], 0.0))

            def add_square(src, m):
                dve.tensor_tensor(sq_t[:, 0:1, :], src, src, ALU.mult).then_inc(S("sq_ready"), 1)
                dve.wait_ge(S("sq_ready"), m + 1)
                dve.tensor_tensor(sq_sum[:, :], sq_sum[:, :], sq_t[:, 0, :], ALU.add).then_inc(S("sq_summed"), 1)

            def add_residual(m, x, s, v=0, k=0):
                tile = res[:, bass.ds(m, 1), :]
                before(dve, chunk_done, s + 1, v, k)
                before(dve, S("xT_copied"), x + 3, v, k // 2)
                dve.tensor_tensor(tile, bank[x % 2][:, None, :], xT_buf[:, x % 2:x % 2 + 1, :], ALU.add).then_inc(S("x1_ready"), 1)
                before(dve, S("x1_ready"), x + 3, v, k // 2)
                add_square(tile, m)

            with dve.Fori(0, 7) as i:
                for x in range(2):
                    add_residual(i * 2 + x, x, C_O + 2 * x + 1, i, 4)
            add_residual(14, 14, C_O + 29)
            split_operand(3, G_X, range(CK))
            add_residual(15, 15, C_O + 31)

            split_operand(3, G_X, range(CK, KT))

            def rstd_rows(n):
                dve.wait_ge(S("x_mean_done"), n + 1)
                dve.tensor_scalar(v_t[:, :], mean_bank[n], 1.0 / D, EPS, ALU.mult, ALU.add).then_inc(S("v_ready"), 1)
                dve.wait_ge(S("rstd_rough"), n + 1)
                dve.wait_ge(S("v_ready"), n + 1)
                newton(v_t[:, :], rstd_t[:, :], n_t[:, :], "rstd_x")
                dve.wait_ge(S("rstd_x"), n + 1)

            rstd_rows(0)
            def x_out_lo(h):
                dve.wait_ge(S("o_hi_ready"), 2 * HEADS + h + 1)
                dve.tensor_tensor(o_lo[:, h, :], bank[7], o_hi[:, h, :].bitcast(F32), ALU.subtract).then_inc(S("o_split"), 1)

            for u in range(XH + 1):
                if u:
                    h = u - 1
                    dve.wait_ge(S("x_scores_done"), h + 1)
                    link(dve.tensor_reduce(x_small[:, 2, :], psum[:, 2:4].rearrange("p b (t k) -> p (b t) k", t=2), AX.X, ALU.max))
                    dve.tensor_scalar(x_small[:, 0, :], x_small[:, 2, :], -X_SCALE, None, ALU.mult).then_inc(S("x_max"), 1)
                    dve.wait_ge(S("x_probs_done"), h + 1)
                    link(dve.reciprocal(x_small[:, 2, :], x_small[:, 1, :]))
                    dve.tensor_tensor(p_x[:, :, :], p_x[:, :, :], x_small[:, 2, :, None].to_broadcast([P, TT, M]), ALU.mult).then_inc(S("x_probs_ready"), 1)
                if u >= 2:
                    x_out_lo(u - 2)
                if u < XH:
                    done(C_XQ + 2 * u + 1)
                    dve.tensor_tensor(q_x[:, u, :], bank[u % 2], rstd_t[:, :], ALU.mult).then_inc(S("q_scaled"), 1)
            x_out_lo(XH - 1)
            link(dve.memset(sq_sum[:, :], 0.0))
            for s in range(8):
                done(C_XO + s)
                for m in range(2 * s, 2 * s + 2):
                    dve.tensor_tensor(res[:, m, :], bank[m % 4], res[:, m, :], ALU.add).then_inc(S("x2_ready"), 1)
                split_operand(4, G_FFN, range(2 * s, 2 * s + 2))
                for m in range(2 * s, 2 * s + 2):
                    dve.wait_ge(S("sq_ready"), KT + m + 1)
                    dve.wait_ge(S("sq_summed"), KT + m)
                    dve.tensor_tensor(sq_sum[:, :], sq_sum[:, :], sq_t[:, m % 2, :], ALU.add).then_inc(S("sq_summed"), 1)

            done(C_XO + 7)
            for kt in range(1, KT, 2):
                dve.wait_ge(S("x2_turned"), kt + 1)
                dve.tensor_copy(x2_nat[:, :, kt * P:(kt + 1) * P], bank[4 + kt % 4].rearrange("p (t d) -> p t d", t=TT)).then_inc(S("x2_nat_ready1"), 1)
            rstd_rows(1)

            def ffn_up(v, k):
                for f in range(FB):
                    done(C_F + 4 * f + 1, v, k)
                    dve.tensor_tensor(g1_t[:, :], bank[0], rstd_t[:, :], ALU.mult).then_inc(S("gate_scaled"), 1)
                    done(C_F + 4 * f + 3, v, k)
                    dve.tensor_tensor(u1_t[:, :], bank[1], rstd_t[:, :], ALU.mult).then_inc(S("up_scaled"), 1)
                    before(dve, S("ffn_sig"), f + 1, v, FB)
                    dve.tensor_tensor(g1_t[:, :], g1_t[:, :], sg_t[:, :], ALU.mult).then_inc(S("ffn_silu"), 1)
                    before(dve, S("ffn_silu"), f + 1, v, FB)
                    before(dve, S("up_scaled"), f + 1, v, FB)
                    dve.tensor_tensor(a_t[:, :], g1_t[:, :], u1_t[:, :], ALU.mult).then_inc(S("a_ready"), 1)
                    before(dve, S("a_hi_ready"), f + 1, v, FB)
                    before(dve, S("a_ready"), f + 1, v, FB)
                    dve.tensor_tensor(a_lo[:, f, :], a_t[:, :], a_hi[:, f, :].bitcast(F32), ALU.subtract).then_inc(S("a_split"), 1)

            def ffn_down(v, k):
                for d in range(4):
                    banks = (2, 3, 4, 5) if d % 2 == 0 else (0, 1, 6, 7)
                    for t in range(TT):
                        if t < TT - 1:
                            before(dve, S("down_tile_done"), 3 * d + t + 1, v, 12)
                        else:
                            done(C_F + 16 + 2 * d + 1, v, k)
                        o = x2_nat[:, t, d * 512:(d + 1) * 512]
                        dve.tensor_tensor(o, o, bank[banks[t]], ALU.add).then_inc(S("down_added"), 1)

            for x in range(2):
                dve.wait_ge(S(f"x2_nat_ready{x}"), KT // 2)
            with dve.Fori(0, NFB - 1) as b:
                ffn_up(b, CF_BLOCK)
                ffn_down(b, CF_BLOCK)
            ffn_up(NFB - 1, CF_BLOCK)
            dve.wait_ge(S("g_final_in"), 16)

            def piece(n):
                t, d, _ = LAST_GROUPS[n]
                return x2_nat[:, t, d * 512:(d + 1) * 512], g_final[:, d * 512:(d + 1) * 512]

            for n, (t, d, b) in enumerate(LAST_GROUPS):
                o, gain = piece(n)
                dve.wait_ge(S("last_group_done"), n + 1)
                dve.tensor_tensor(o, o, bank[b], ALU.add).then_inc(S("down_added"), 1)
                if n - 1 in GAINED:
                    o_before, gain_before = piece(n - 1)
                    dve.wait_ge(S("final_squared"), n)
                    dve.tensor_tensor(o_before, o_before, gain_before, ALU.mult).then_inc(S("gain_applied"), 1)
                if d == 3:
                    total, v, r, tmp = [f_stat[:, x, t:t + 1] for x in (0, 1, 3, 4)]
                    dve.wait_ge(S("final_squared"), n + 1)
                    link(dve.tensor_reduce(total, f_squares[:, t, :], AX.X, ALU.add))
                    dve.tensor_scalar(v, total, 1.0 / D, EPS, ALU.mult, ALU.add).then_inc(S("final_v"), 1)
                    dve.wait_ge(S("final_rough"), t + 1)
                    newton(v, r, tmp, "final_rstd")
                    dve.wait_ge(S("final_rstd"), t + 1)
                    dve.scalar_tensor_tensor(o, o, r, gain, ALU.mult, ALU.mult).then_inc(S("dve_out_ready"), 1)


_INS = ["x", "mem", "positions", "norm_mix", "w_in", "hg_lower", "hg_norm", "sw_sinks", "w_proj_a", "w_proj_b",
        "w_out", "norm_x", "norm_mem", "wq_x", "wk_x", "wv_x", "wo_x", "norm_ffn", "w_gate", "w_up", "w_down",
        "norm_final"]


def constants():
    import numpy as np

    consts = np.zeros((P, P + T + 2), np.float32)
    consts[:, 0:P] = np.eye(P)
    consts[:, P:P + T] = np.arange(T) % BLK != 0
    half = HD // 2
    j = np.arange(P) % half
    consts[:, P + T] = np.float32(10000.0) ** (-j.astype(np.float32) / np.float32(half))
    consts[:, P + T + 1] = np.where(np.arange(P) % HD < half, -1.0, 1.0)
    masks = np.zeros((P, NL, BLK // 2), np.int32)
    s, t = np.arange(BLK)[:, None], np.arange(BLK)[None, :]
    for n, w in enumerate(LEVELS):
        pairs = (s // (2 * w) == t // (2 * w)) & (s % (2 * w) < w)
        masks[:, n] = pairs[:, t[0] % (2 * w) >= w]
    return {"consts": consts, "masks": masks}


def kernel(**inputs):
    import numpy as np
    import concourse.bacc as bacc
    from concourse.bass_utils import run_bass_kernel_spmd

    nc = bacc.Bacc("TRN2", target_bir_lowering=False, num_devices=1)
    arrays = {name: np.ascontiguousarray(inputs[name]) for name in _INS}
    arrays.update(constants())
    feed, args = {}, {}
    for name, array in arrays.items():
        feed["in_" + name] = array
        args[name] = nc.dram_tensor("in_" + name, array.shape, mybir.dt.from_np(array.dtype), kind="ExternalInput").ap()
    result = nc.dram_tensor("out", (1, T, D), F32, kind="ExternalOutput").ap()
    build_trunk(nc, args, result)
    return run_bass_kernel_spmd(nc, [feed], core_ids=[0]).results[0]["out"]
```
